# Optimizing a Trainium2 kernel written in Bass

```python
import jax, jax.numpy as jnp
from jax import lax
import numpy as np

D_MODEL = 1024
BATCH = 1
SEQ = 512
DEPTH = 1

D_RNN = D_MODEL
RG_HEADS = 4
RG_BLOCK = D_RNN // RG_HEADS
RG_C = 8.0
CONV4_WIDTH = 4
D_CONV = D_MODEL
CONV3_WIDTH = 3
D_FF = ((8 * D_MODEL + 3 * 256 - 1) // (3 * 256)) * 256
PLE_DIM = 256
EPS = 1e-6
IN_SPLITS = (D_RNN, D_RNN, D_CONV, D_CONV, D_CONV, D_MODEL, D_MODEL)
W_IN = sum(IN_SPLITS)
IN_OFFSETS = tuple(int(v) for v in np.cumsum(IN_SPLITS)[:-1])


def rmsnorm(x, g):
    xf = x.astype(jnp.float32)
    y = xf * lax.rsqrt(jnp.mean(xf * xf, axis=-1, keepdims=True) + EPS)
    return (y * g.astype(jnp.float32)).astype(x.dtype)

def causal_depthwise_conv(x, w):
    k_w = w.shape[0]
    t = x.shape[1]
    xp = jnp.pad(x, ((0, 0), (k_w - 1, 0), (0, 0)))
    y = xp[:, 0:t] * w[0]
    for k in range(1, k_w):
        y = y + xp[:, k:k + t] * w[k]
    return y

def block_diag_linear(x, w, b):
    bsz, t, _ = x.shape
    xh = x.reshape(bsz, t, RG_HEADS, RG_BLOCK)
    y = jnp.einsum("bthi,hij->bthj", xh, w) + b
    return y.reshape(bsz, t, RG_HEADS * RG_BLOCK)

def rg_lru(x, w_r, b_r, w_i, b_i, lam):
    r = jax.nn.sigmoid(block_diag_linear(x, w_r, b_r).astype(jnp.float32))
    i = jax.nn.sigmoid(block_diag_linear(x, w_i, b_i).astype(jnp.float32))
    log_a = -RG_C * r * jax.nn.softplus(-lam.astype(jnp.float32))
    a = jnp.exp(log_a)
    mult = jnp.sqrt(-jnp.expm1(2.0 * log_a))
    u = mult * (i * x.astype(jnp.float32))

    def step(h, au):
        a_t, u_t = au
        h = a_t * h + u_t
        return h, h

    h0 = jnp.zeros((x.shape[0], x.shape[2]), jnp.float32)
    _, hs = lax.scan(step, h0, (jnp.swapaxes(a, 0, 1), jnp.swapaxes(u, 0, 1)))
    return jnp.swapaxes(hs, 0, 1).astype(x.dtype)

def hybrid_layer(x, p_i, g_mix, w_in, conv4_w, conv4_b, w_rg_r, b_rg_r, w_rg_i, b_rg_i,
                 lru_lambda, conv3_w, w_out, g_ffn, w_gate_up, w_down, g_ple, w_ple_gate, w_ple):
    h = rmsnorm(x, g_mix)
    z = h @ w_in
    rnn_x, rnn_y, conv_b, conv_c, conv_x, gate_rnn, gate_conv = jnp.split(z, IN_OFFSETS, axis=-1)
    rnn_x = causal_depthwise_conv(rnn_x, conv4_w) + conv4_b
    y_rnn = jax.nn.gelu(rnn_y) * rg_lru(rnn_x, w_rg_r, b_rg_r, w_rg_i, b_rg_i, lru_lambda)
    y_conv = conv_b * causal_depthwise_conv(conv_c * conv_x, conv3_w)
    merged = jax.nn.sigmoid(gate_rnn) * y_rnn + jax.nn.sigmoid(gate_conv) * y_conv
    x = x + merged @ w_out
    h = rmsnorm(x, g_ffn)
    g, u = jnp.split(h @ w_gate_up, 2, axis=-1)
    x = x + (jax.nn.silu(g) * u) @ w_down
    gate = jax.nn.sigmoid(rmsnorm(x, g_ple) @ w_ple_gate)
    x = x + gate * (p_i @ w_ple)
    return x

def first_inputs(seed: int = 0) -> dict:
    key = jax.random.key(seed)
    ks = jax.random.split(key, 20)

    def nrm(k, shape, fan_in):
        return jax.random.normal(k, shape, jnp.float32) * (fan_in ** -0.5)

    def gain(k, shape):
        return 1.0 + 0.05 * jax.random.normal(k, shape, jnp.float32)

    def bias(k, shape):
        return 0.02 * jax.random.normal(k, shape, jnp.float32)

    x = jax.random.normal(ks[0], (BATCH, SEQ, D_MODEL), jnp.float32)
    p = jax.random.normal(ks[1], (DEPTH, BATCH, SEQ, PLE_DIM), jnp.float32)
    g_mix = gain(ks[2], (DEPTH, D_MODEL))
    w_in = nrm(ks[3], (DEPTH, D_MODEL, W_IN), D_MODEL)
    conv4_w = nrm(ks[4], (DEPTH, CONV4_WIDTH, D_RNN), CONV4_WIDTH)
    conv4_b = bias(ks[5], (DEPTH, D_RNN))
    w_rg_r = nrm(ks[6], (DEPTH, RG_HEADS, RG_BLOCK, RG_BLOCK), RG_BLOCK)
    b_rg_r = bias(ks[7], (DEPTH, RG_HEADS, RG_BLOCK))
    w_rg_i = nrm(ks[8], (DEPTH, RG_HEADS, RG_BLOCK, RG_BLOCK), RG_BLOCK)
    b_rg_i = bias(ks[9], (DEPTH, RG_HEADS, RG_BLOCK))
    a_c = jax.random.uniform(ks[10], (DEPTH, D_RNN), jnp.float32, minval=0.9, maxval=0.999)
    a0 = a_c ** (1.0 / RG_C)
    lru_lambda = jnp.log(a0) - jnp.log1p(-a0)
    conv3_w = nrm(ks[11], (DEPTH, CONV3_WIDTH, D_CONV), CONV3_WIDTH)
    w_out = nrm(ks[12], (DEPTH, D_MODEL, D_MODEL), D_MODEL)
    g_ffn = gain(ks[13], (DEPTH, D_MODEL))
    w_gate_up = nrm(ks[14], (DEPTH, D_MODEL, 2 * D_FF), D_MODEL)
    w_down = nrm(ks[15], (DEPTH, D_FF, D_MODEL), D_FF)
    g_ple = gain(ks[16], (DEPTH, D_MODEL))
    w_ple_gate = nrm(ks[17], (DEPTH, D_MODEL, D_MODEL), D_MODEL)
    w_ple = nrm(ks[18], (DEPTH, PLE_DIM, D_MODEL), PLE_DIM)
    g_final = gain(ks[19], (D_MODEL,))
    return {"x": x, "p": p, "g_mix": g_mix, "w_in": w_in, "conv4_w": conv4_w,
            "conv4_b": conv4_b, "w_rg_r": w_rg_r, "b_rg_r": b_rg_r, "w_rg_i": w_rg_i,
            "b_rg_i": b_rg_i, "lru_lambda": lru_lambda, "conv3_w": conv3_w, "w_out": w_out,
            "g_ffn": g_ffn, "w_gate_up": w_gate_up, "w_down": w_down, "g_ple": g_ple,
            "w_ple_gate": w_ple_gate, "w_ple": w_ple, "g_final": g_final}

def first_block(x, p, g_mix, w_in, conv4_w, conv4_b, w_rg_r, b_rg_r, w_rg_i, b_rg_i,
              lru_lambda, conv3_w, w_out, g_ffn, w_gate_up, w_down, g_ple, w_ple_gate,
              w_ple, g_final):
    for i in range(DEPTH):
        x = hybrid_layer(x, p[i], g_mix[i], w_in[i], conv4_w[i], conv4_b[i], w_rg_r[i],
                         b_rg_r[i], w_rg_i[i], b_rg_i[i], lru_lambda[i], conv3_w[i], w_out[i],
                         g_ffn[i], w_gate_up[i], w_down[i], g_ple[i], w_ple_gate[i], w_ple[i])
    return rmsnorm(x, g_final)


NEG_INF = -1e30
FORCE_SCORE = 1e9
ROPE_THETA = 500000.0
Q_BLOCK = 128

A_HEADS = 8
A_KV_HEADS = 2
A_HEAD_DIM = 64
A_ROPE_DIM = A_HEAD_DIM // 4
CMP_LEN = 32
CMP_STRIDE = 16
CMP_HIDDEN = 256
SLC_LEN = 64
SLC_TOPK = 16
WINDOW = 512
A_WIDTH = A_HEADS * A_HEAD_DIM
A_KV_WIDTH = A_KV_HEADS * A_HEAD_DIM

B_HEADS = 8
Q_LORA = 256
KV_LORA = 128
B_NOPE = 64
B_ROPE = 32
B_V = 64
B_QK = B_NOPE + B_ROPE
B_WIDTH = B_HEADS * B_V

MIX_WIDTH = A_WIDTH + B_WIDTH
IN_SIZES = (A_WIDTH, A_KV_WIDTH, A_KV_WIDTH, A_KV_WIDTH, A_KV_WIDTH, A_KV_WIDTH, A_KV_WIDTH,
            3 * A_HEADS, Q_LORA, KV_LORA, B_ROPE)
IN_WIDTH = sum(IN_SIZES)

P_HEADS = 8
N_KEYS = 128
N_EXPERTS = N_KEYS * N_KEYS
P_KEY_DIM = 256
P_TOPK = 16
P_CHUNK = 128


def _rms(x):
    xf = x.astype(jnp.float32)
    return xf * lax.rsqrt(jnp.mean(xf * xf, axis=-1, keepdims=True) + EPS)

def rmsnorm_2(x, gain):
    return (_rms(x) * gain.astype(jnp.float32)).astype(x.dtype)

def rope_tables(pos, rot_dim):
    inv_freq = ROPE_THETA ** (-jnp.arange(0, rot_dim, 2, dtype=jnp.float32) / rot_dim)
    ang = pos.astype(jnp.float32)[..., None] * inv_freq
    return jnp.cos(ang), jnp.sin(ang)

def apply_rope(x, cos, sin):
    half = cos.shape[-1]
    xf = x.astype(jnp.float32)
    x1, x2, rest = xf[..., :half], xf[..., half:2 * half], xf[..., 2 * half:]
    out = jnp.concatenate([x1 * cos - x2 * sin, x2 * cos + x1 * sin, rest], axis=-1)
    return out.astype(x.dtype)

def masked_softmax(s, mask):
    s = jnp.where(mask, s.astype(jnp.float32), NEG_INF)
    p = jax.nn.softmax(s, axis=-1)
    return jnp.where(mask, p, 0.0)

def nsa_mixer(q, k_cmp, v_cmp, k_slc, v_slc, k_win, v_win, gates, positions,
              q_gain, kc_gain, ks_gain, kw_gain, cmp_pos, cmp_k_w1, cmp_k_w2, cmp_v_w1, cmp_v_w2):
    B, S = q.shape[:2]
    G, R, dk = A_KV_HEADS, A_HEADS // A_KV_HEADS, A_HEAD_DIM
    scale = dk ** -0.5
    cos, sin = rope_tables(positions, A_ROPE_DIM)
    cos_h, sin_h = cos[:, :, None, :], sin[:, :, None, :]
    q = apply_rope(rmsnorm_2(q, q_gain), cos_h, sin_h)
    k_slc = apply_rope(rmsnorm_2(k_slc, ks_gain), cos_h, sin_h)
    k_win = apply_rope(rmsnorm_2(k_win, kw_gain), cos_h, sin_h)

    n_cmp = (S - CMP_LEN) // CMP_STRIDE + 1
    cmp_idx = jnp.arange(n_cmp)[:, None] * CMP_STRIDE + jnp.arange(CMP_LEN)[None, :]
    cmp_start, cmp_end = cmp_idx[:, 0], cmp_idx[:, -1]

    def compress(t, w1, w2):
        blk = t[:, cmp_idx] + cmp_pos[:, None, :]
        blk = blk.transpose(0, 1, 3, 2, 4).reshape(B, n_cmp, G, CMP_LEN * dk)
        return jax.nn.gelu(blk @ w1) @ w2

    kc = compress(k_cmp, cmp_k_w1, cmp_k_w2)
    vc = compress(v_cmp, cmp_v_w1, cmp_v_w2)
    cos_c, sin_c = rope_tables(positions[:, cmp_end], A_ROPE_DIM)
    kc = apply_rope(rmsnorm_2(kc, kc_gain), cos_c[:, :, None, :], sin_c[:, :, None, :])

    n_slc = S // SLC_LEN
    topk = min(SLC_TOPK, n_slc)
    slc_start = jnp.arange(n_slc) * SLC_LEN
    overlap = ((cmp_start[:, None] < slc_start[None, :] + SLC_LEN)
               & (cmp_end[:, None] >= slc_start[None, :])).astype(jnp.float32)
    ks_blocks = k_slc.reshape(B, n_slc, SLC_LEN, G, dk).transpose(0, 3, 1, 2, 4)
    vs_blocks = v_slc.reshape(B, n_slc, SLC_LEN, G, dk).transpose(0, 3, 1, 2, 4)

    pad = ((0, 0), (WINDOW, 0), (0, 0), (0, 0))
    kw_pad, vw_pad = jnp.pad(k_win, pad), jnp.pad(v_win, pad)

    def block(qb):
        q0 = qb * Q_BLOCK
        t = q0 + jnp.arange(Q_BLOCK)
        qblk = lax.dynamic_slice_in_dim(q, q0, Q_BLOCK, axis=1).reshape(B, Q_BLOCK, G, R, dk)
        gblk = lax.dynamic_slice_in_dim(gates, q0, Q_BLOCK, axis=1).reshape(B, Q_BLOCK, G, R, 3)

        s_c = jnp.einsum('bqgrd,bngd->bgrqn', qblk, kc) * scale
        p_c = masked_softmax(s_c, cmp_end[None, :] <= t[:, None])
        o_c = jnp.einsum('bgrqn,bngd->bqgrd', p_c.astype(vc.dtype), vc)

        imp = jnp.einsum('bgrqn,nj->bgqj', p_c, overlap)
        j = jnp.arange(n_slc)
        forced = (j[None, :] == (t // SLC_LEN)[:, None]) | (j[None, :] == 0)
        causal_blk = slc_start[None, :] <= t[:, None]
        imp = jnp.where(forced, FORCE_SCORE, jnp.where(causal_blk, imp, NEG_INF))
        _, sel = lax.top_k(imp, topk)
        flat = sel.reshape(B, G, Q_BLOCK * topk)[..., None, None]
        ks = jnp.take_along_axis(ks_blocks, flat, axis=2).reshape(B, G, Q_BLOCK, topk * SLC_LEN, dk)
        vs = jnp.take_along_axis(vs_blocks, flat, axis=2).reshape(B, G, Q_BLOCK, topk * SLC_LEN, dk)
        tok = (sel[..., None] * SLC_LEN + jnp.arange(SLC_LEN)).reshape(B, G, Q_BLOCK, topk * SLC_LEN)
        mask_s = (tok <= t[:, None])[:, :, None]
        s_s = jnp.einsum('bqgrd,bgqsd->bgrqs', qblk, ks) * scale
        p_s = masked_softmax(s_s, mask_s)
        o_s = jnp.einsum('bgrqs,bgqsd->bqgrd', p_s.astype(vs.dtype), vs)

        kw = lax.dynamic_slice_in_dim(kw_pad, q0, Q_BLOCK + WINDOW, axis=1)
        vw = lax.dynamic_slice_in_dim(vw_pad, q0, Q_BLOCK + WINDOW, axis=1)
        s_pos = q0 - WINDOW + jnp.arange(Q_BLOCK + WINDOW)
        mask_w = ((s_pos[None, :] <= t[:, None]) & (s_pos[None, :] > t[:, None] - WINDOW)
                  & (s_pos[None, :] >= 0))
        s_w = jnp.einsum('bqgrd,bsgd->bgrqs', qblk, kw) * scale
        p_w = masked_softmax(s_w, mask_w)
        o_w = jnp.einsum('bgrqs,bsgd->bqgrd', p_w.astype(vw.dtype), vw)

        return gblk[..., 0:1] * o_c + gblk[..., 1:2] * o_s + gblk[..., 2:3] * o_w

    out = lax.map(block, jnp.arange(S // Q_BLOCK))
    return out.transpose(1, 0, 2, 3, 4, 5).reshape(B, S, A_WIDTH)

def mla_mixer(c_q, c_kv, k_rope, positions, q_lora_gain, w_uq, kv_lora_gain, w_ukv, q_gain, k_gain):
    B, S = c_q.shape[:2]
    H = B_HEADS
    cos, sin = rope_tables(positions, B_ROPE)
    cos_h, sin_h = cos[:, :, None, :], sin[:, :, None, :]
    q = (rmsnorm_2(c_q, q_lora_gain) @ w_uq).reshape(B, S, H, B_QK)
    kv = (rmsnorm_2(c_kv, kv_lora_gain) @ w_ukv).reshape(B, S, H, B_NOPE + B_V)
    k_nope, v = kv[..., :B_NOPE], kv[..., B_NOPE:]
    k = jnp.concatenate([k_nope, jnp.broadcast_to(k_rope[:, :, None, :], (B, S, H, B_ROPE))], axis=-1)
    q, k = rmsnorm_2(q, q_gain), rmsnorm_2(k, k_gain)
    q = jnp.concatenate([q[..., :B_NOPE], apply_rope(q[..., B_NOPE:], cos_h, sin_h)], axis=-1)
    k = jnp.concatenate([k[..., :B_NOPE], apply_rope(k[..., B_NOPE:], cos_h, sin_h)], axis=-1)
    scale = B_QK ** -0.5
    key_idx = jnp.arange(S)

    def block(qb):
        q0 = qb * Q_BLOCK
        t = q0 + jnp.arange(Q_BLOCK)
        qblk = lax.dynamic_slice_in_dim(q, q0, Q_BLOCK, axis=1)
        s = jnp.einsum('bqhd,bshd->bhqs', qblk, k) * scale
        p = masked_softmax(s, key_idx[None, :] <= t[:, None])
        return jnp.einsum('bhqs,bshd->bqhd', p.astype(v.dtype), v)

    out = lax.map(block, jnp.arange(S // Q_BLOCK))
    return out.transpose(1, 0, 2, 3, 4).reshape(B, S, B_WIDTH)

def peer_ffn(x, w_q, sub_keys, expert_u, expert_v):
    B, S, D = x.shape
    T = B * S
    xt = x.reshape(T, D)
    q = _rms((xt @ w_q).reshape(T, P_HEADS, P_KEY_DIM)).astype(x.dtype)
    half = P_KEY_DIM // 2
    s1 = jnp.einsum('thd,hnd->thn', q[..., :half], sub_keys[:, 0]).astype(jnp.float32)
    s2 = jnp.einsum('thd,hnd->thn', q[..., half:], sub_keys[:, 1]).astype(jnp.float32)
    v1, i1 = lax.top_k(s1, P_TOPK)
    v2, i2 = lax.top_k(s2, P_TOPK)
    cand = (v1[..., :, None] + v2[..., None, :]).reshape(T, P_HEADS, P_TOPK * P_TOPK)
    vals, ci = lax.top_k(cand, P_TOPK)
    e = (jnp.take_along_axis(i1, ci // P_TOPK, axis=-1) * N_KEYS
         + jnp.take_along_axis(i2, ci % P_TOPK, axis=-1))
    g = jax.nn.softmax(vals, axis=-1)
    n_chunks = T // P_CHUNK

    def chunk(args):
        xc, ec, gc = args
        a = jnp.einsum('cd,ckd->ck', xc, expert_u[ec])
        w = (gc * jax.nn.gelu(a.astype(jnp.float32))).astype(x.dtype)
        return jnp.einsum('ck,ckd->cd', w, expert_v[ec])

    y = lax.map(chunk, (xt.reshape(n_chunks, P_CHUNK, D),
                        e.reshape(n_chunks, P_CHUNK, P_HEADS * P_TOPK),
                        g.reshape(n_chunks, P_CHUNK, P_HEADS * P_TOPK)))
    return y.reshape(B, S, D)

def hybrid_layer_2(x, positions, norm1_gain, w_in,
                 nsa_q_gain, nsa_kc_gain, nsa_ks_gain, nsa_kw_gain,
                 cmp_pos, cmp_k_w1, cmp_k_w2, cmp_v_w1, cmp_v_w2,
                 mla_q_lora_gain, mla_w_uq, mla_kv_lora_gain, mla_w_ukv, mla_q_gain, mla_k_gain,
                 out_gain_a, out_gain_b, w_out,
                 norm2_gain, peer_w_q, peer_sub_keys, peer_u, peer_v):
    B, S, _ = x.shape
    proj = rmsnorm_2(x, norm1_gain) @ w_in
    pts = [int(p) for p in np.cumsum(IN_SIZES)[:-1]]
    (a_q, a_kc, a_vc, a_ks, a_vs, a_kw, a_vw, a_gate, b_cq, b_ckv, b_kr) = jnp.split(proj, pts, axis=-1)
    kvs = lambda t: t.reshape(B, S, A_KV_HEADS, A_HEAD_DIM)
    gates = jax.nn.sigmoid(a_gate).reshape(B, S, A_HEADS, 3)
    o_a = nsa_mixer(a_q.reshape(B, S, A_HEADS, A_HEAD_DIM), kvs(a_kc), kvs(a_vc), kvs(a_ks), kvs(a_vs),
                    kvs(a_kw), kvs(a_vw), gates, positions,
                    nsa_q_gain, nsa_kc_gain, nsa_ks_gain, nsa_kw_gain,
                    cmp_pos, cmp_k_w1, cmp_k_w2, cmp_v_w1, cmp_v_w2)
    o_b = mla_mixer(b_cq, b_ckv, b_kr, positions, mla_q_lora_gain, mla_w_uq,
                    mla_kv_lora_gain, mla_w_ukv, mla_q_gain, mla_k_gain)
    mixed = jnp.concatenate([rmsnorm_2(o_a, out_gain_a), rmsnorm_2(o_b, out_gain_b)], axis=-1) @ w_out
    h = x + mixed
    return h + peer_ffn(rmsnorm_2(h, norm2_gain), peer_w_q, peer_sub_keys, peer_u, peer_v)

def second_inputs(seed: int = 0) -> dict:
    key = jax.random.key(seed)
    ks = jax.random.split(key, 32)
    L = DEPTH
    nrm = lambda k, shape, s: jax.random.normal(k, shape, jnp.float32) * s
    gain = lambda k, n: 1.0 + 0.02 * jax.random.normal(k, (L, n), jnp.float32)
    start = jax.random.randint(ks[1], (BATCH, 1), 0, 4096, dtype=jnp.int32)
    return {
        'x': nrm(ks[0], (BATCH, SEQ, D_MODEL), 1.0),
        'positions': (start + jnp.arange(SEQ, dtype=jnp.int32)[None, :]).astype(jnp.int32),
        'norm1_gain': gain(ks[2], D_MODEL),
        'w_in': nrm(ks[3], (L, D_MODEL, IN_WIDTH), D_MODEL ** -0.5),
        'nsa_q_gain': gain(ks[4], A_HEAD_DIM),
        'nsa_kc_gain': gain(ks[5], A_HEAD_DIM),
        'nsa_ks_gain': gain(ks[6], A_HEAD_DIM),
        'nsa_kw_gain': gain(ks[7], A_HEAD_DIM),
        'cmp_pos': nrm(ks[8], (L, CMP_LEN, A_HEAD_DIM), 0.1),
        'cmp_k_w1': nrm(ks[9], (L, CMP_LEN * A_HEAD_DIM, CMP_HIDDEN), (CMP_LEN * A_HEAD_DIM) ** -0.5),
        'cmp_k_w2': nrm(ks[10], (L, CMP_HIDDEN, A_HEAD_DIM), CMP_HIDDEN ** -0.5),
        'cmp_v_w1': nrm(ks[11], (L, CMP_LEN * A_HEAD_DIM, CMP_HIDDEN), (CMP_LEN * A_HEAD_DIM) ** -0.5),
        'cmp_v_w2': nrm(ks[12], (L, CMP_HIDDEN, A_HEAD_DIM), CMP_HIDDEN ** -0.5),
        'mla_q_lora_gain': gain(ks[13], Q_LORA),
        'mla_w_uq': nrm(ks[14], (L, Q_LORA, B_HEADS * B_QK), Q_LORA ** -0.5),
        'mla_kv_lora_gain': gain(ks[15], KV_LORA),
        'mla_w_ukv': nrm(ks[16], (L, KV_LORA, B_HEADS * (B_NOPE + B_V)), KV_LORA ** -0.5),
        'mla_q_gain': gain(ks[17], B_QK),
        'mla_k_gain': gain(ks[18], B_QK),
        'out_gain_a': gain(ks[19], A_WIDTH),
        'out_gain_b': gain(ks[20], B_WIDTH),
        'w_out': nrm(ks[21], (L, MIX_WIDTH, D_MODEL), MIX_WIDTH ** -0.5),
        'norm2_gain': gain(ks[22], D_MODEL),
        'peer_w_q': nrm(ks[23], (L, D_MODEL, P_HEADS * P_KEY_DIM), D_MODEL ** -0.5),
        'peer_sub_keys': nrm(ks[24], (L, P_HEADS, 2, N_KEYS, P_KEY_DIM // 2), (P_KEY_DIM // 2) ** -0.5),
        'peer_u': nrm(ks[25], (L, N_EXPERTS, D_MODEL), D_MODEL ** -0.5),
        'peer_v': nrm(ks[26], (L, N_EXPERTS, D_MODEL), D_MODEL ** -0.5),
    }

def second_block(x, positions, norm1_gain, w_in,
              nsa_q_gain, nsa_kc_gain, nsa_ks_gain, nsa_kw_gain,
              cmp_pos, cmp_k_w1, cmp_k_w2, cmp_v_w1, cmp_v_w2,
              mla_q_lora_gain, mla_w_uq, mla_kv_lora_gain, mla_w_ukv, mla_q_gain, mla_k_gain,
              out_gain_a, out_gain_b, w_out,
              norm2_gain, peer_w_q, peer_sub_keys, peer_u, peer_v):
    h = x
    for l in range(DEPTH):
        h = hybrid_layer_2(h, positions, norm1_gain[l], w_in[l],
                         nsa_q_gain[l], nsa_kc_gain[l], nsa_ks_gain[l], nsa_kw_gain[l],
                         cmp_pos[l], cmp_k_w1[l], cmp_k_w2[l], cmp_v_w1[l], cmp_v_w2[l],
                         mla_q_lora_gain[l], mla_w_uq[l], mla_kv_lora_gain[l], mla_w_ukv[l],
                         mla_q_gain[l], mla_k_gain[l],
                         out_gain_a[l], out_gain_b[l], w_out[l],
                         norm2_gain[l], peer_w_q[l], peer_sub_keys[l], peer_u[l], peer_v[l])
    return h


def setup_inputs(seed=0):
    out = dict(first_inputs(seed))
    for name, value in second_inputs(seed + 1).items():
        if name != "x":
            out[name + "_2"] = value
    return out


def reference(
    x, p, g_mix, w_in, conv4_w, conv4_b, w_rg_r, b_rg_r, w_rg_i, b_rg_i, lru_lambda, conv3_w,
    w_out, g_ffn, w_gate_up, w_down, g_ple, w_ple_gate, w_ple, g_final, positions_2,
    norm1_gain_2, w_in_2, nsa_q_gain_2, nsa_kc_gain_2, nsa_ks_gain_2, nsa_kw_gain_2, cmp_pos_2,
    cmp_k_w1_2, cmp_k_w2_2, cmp_v_w1_2, cmp_v_w2_2, mla_q_lora_gain_2, mla_w_uq_2,
    mla_kv_lora_gain_2, mla_w_ukv_2, mla_q_gain_2, mla_k_gain_2, out_gain_a_2, out_gain_b_2,
    w_out_2, norm2_gain_2, peer_w_q_2, peer_sub_keys_2, peer_u_2, peer_v_2,
):
    x = first_block(
        x, p, g_mix, w_in, conv4_w, conv4_b, w_rg_r, b_rg_r, w_rg_i, b_rg_i, lru_lambda,
        conv3_w, w_out, g_ffn, w_gate_up, w_down, g_ple, w_ple_gate, w_ple, g_final,
    )
    return second_block(
        x, positions_2, norm1_gain_2, w_in_2, nsa_q_gain_2, nsa_kc_gain_2, nsa_ks_gain_2,
        nsa_kw_gain_2, cmp_pos_2, cmp_k_w1_2, cmp_k_w2_2, cmp_v_w1_2, cmp_v_w2_2,
        mla_q_lora_gain_2, mla_w_uq_2, mla_kv_lora_gain_2, mla_w_ukv_2, mla_q_gain_2,
        mla_k_gain_2, out_gain_a_2, out_gain_b_2, w_out_2, norm2_gain_2, peer_w_q_2,
        peer_sub_keys_2, peer_u_2, peer_v_2,
    )


_drawn_inputs = setup_inputs


def setup_inputs(seed=0):
    import zlib

    import numpy as np

    out = dict(_drawn_inputs(seed))
    spreads = {}
    factors = {'b_rg_r': 8.0,
     'b_rg_i': 8.0,
     'g_ple': 6.576,
     'norm1_gain_2': 3.051,
     'nsa_q_gain_2': 8.0,
     'nsa_kc_gain_2': 8.0,
     'nsa_ks_gain_2': 8.0,
     'nsa_kw_gain_2': 8.0,
     'mla_q_lora_gain_2': 5.869,
     'mla_kv_lora_gain_2': 5.195,
     'mla_q_gain_2': 6.182,
     'mla_k_gain_2': 5.782,
     'out_gain_a_2': 5.44,
     'out_gain_b_2': 5.339,
     'norm2_gain_2': 8.0,
     'peer_w_q_2': 5.312,
     'peer_sub_keys_2': 5.328,
     'peer_u_2': 5.869,
     'peer_v_2': 5.294}
    for name, (base, spread) in spreads.items():
        noise = np.random.default_rng([zlib.crc32(name.encode()), seed]).standard_normal(out[name].shape)
        drawn = base * np.exp(spread * noise) if base else spread * noise
        out[name] = __import__('jax').numpy.asarray(drawn.astype(out[name].dtype))
    for name, factor in factors.items():
        out[name] = (out[name] * factor).astype(out[name].dtype)
    return out
```

```python
from contextlib import ExitStack

import numpy as np

import concourse.bass as bass
from concourse import mybir

ALU = mybir.AluOpType
ACT = mybir.ActivationFunctionType
F32 = mybir.dt.float32
BF16 = mybir.dt.bfloat16
F32R = mybir.dt.float32r
AX_X = mybir.AxisListType.X

P = 128
T = 512
D = 1024
DC = D // P
EPS = 1e-6
HEADS_RG = 4
BLOCK_RG = D // HEADS_RG
RG_C = 8.0
FF = 2816
FC = FF // P
PLE = 256
A_H, A_G, A_D = 8, 2, 64
A_R = A_H // A_G
A_ROT = 16
CMP_LEN, CMP_STRIDE = 32, 16
N_CMP = (T - CMP_LEN) // CMP_STRIDE + 1
B_H, B_NOPE, B_ROPE, B_V = 8, 64, 32, 64
B_QK = B_NOPE + B_ROPE
Q_LORA = 256
TT = T // P
VW = 2 * A_G * A_D + 3 * A_H
ROPE_THETA = 500000.0
MASKED = -1e30
E_H, E_K, N_KEYS = 8, 16, 128
NEG_HUGE = -3.0e38
assert T // 64 <= 16 and T <= 512
QN = 32
GB = 16
NQ = N_KEYS // QN
HB = 4
E_A = QN
E_Y = QN // 2
E_Q = E_A + 2 * E_Y
EARLY = 24
RING = 4
UNIT = FC // 2 * P

PAR = {}


def _columns():
    at = 0
    for name, n in (("g_mix", DC), ("lam", DC), ("conv4_w", 4 * DC), ("conv4_b", DC), ("b_r", DC), ("b_i", DC),
                    ("conv3_w", 3 * DC), ("g_ffn", DC), ("g_ple", DC), ("g_final", DC), ("eps", 1),
                    ("norm1", DC), ("qk_gain", A_R + 2), ("kc_gain", 1), ("pos_w", CMP_LEN // 2), ("lora_q", 2),
                    ("lora_kv", 1), ("mla_gain", 2 * B_H), ("out_gain", DC), ("norm2", DC)):
        PAR[name] = at
        at += n
    return at


N_PAR = _columns()

U_BLOCK = 0
U_OUT = U_BLOCK + HEADS_RG * 16
U_FF = U_OUT + DC
U_DOWN = U_FF + 2 * FC
U_PLE = U_DOWN + 2 * DC
U_GATE = U_PLE + 2
U_END1 = U_GATE + DC
U_IN2 = U_END1
U_TOK = U_IN2 + 14
U_CMP = U_TOK + 2
U_CMP2 = U_CMP + 8
U_UQ = U_CMP2 + 1
U_UKV = U_UQ + 2
U_OUT2 = U_UKV + 1
U_WQ = U_OUT2 + DC
U_KEYS = U_WQ + 2 * E_H
U_EXP = U_KEYS + 2
N_UNITS = U_EXP

CST = {}


def _cst():
    at = 0
    for name, n in (("ones", P), ("ident", P), ("blk", P), ("rot_a", P), ("rot_b", B_QK), ("causal", P),
                    ("cmp_mask", TT * N_CMP), ("cmp_seen", N_CMP), ("inv_a", 1), ("inv_b", 1), ("iota16", E_K)):
        CST[name] = (at, at + n)
        at += n
    return at


N_CST = _cst()
NORMS = [DC, DC, DC, DC, DC, 2, 1, 4, 4, DC]
NB = [sum(NORMS[:n]) for n in range(len(NORMS) + 1)]

Z_ORDER = [("rx", 0), ("rx", 1), ("ry", 0), ("cb", 0), ("cc", 0), ("cx", 0),
           ("gr", 0), ("gc", 0), ("ry", 1), ("cb", 1), ("cc", 1), ("cx", 1), ("gr", 1), ("gc", 1)]
Z_UNIT = [0, 1, 2, 3, 4, 5, 8, 9, 10, 11, 12, 13, 14, 15]
Z_SPLIT = {"rx": 0, "ry": 1, "cb": 2, "cc": 3, "cx": 4, "gr": 5, "gc": 6}
RG_UNIT = 6
Z_BANKS = 7


class Order:

    def __init__(self, eng, sem):
        self.eng, self.sem, self.base, self.n, self.per = eng, sem, 0, 0, 0

    def __call__(self, ins):
        ins.then_inc(self.sem, 1)
        self.n += 1
        self.eng.wait_ge(self.sem, self.base + self.n)

    def enter(self, i, per):
        self.start, self.per = self.base + self.n, per
        self.base, self.n = i * per + self.start, 0

    def leave(self, passes):
        assert self.n == self.per, self.n
        self.base, self.n = self.start + passes * self.per, 0


def build(nc, xT_in, par_in, pT_in, cst_in, stream, pos_in, u_in, v_in, out):
    with ExitStack() as ctx:
        def sb(name, shape, dt=F32, c=ctx):
            return c.enter_context(nc.sbuf_tensor(name, shape, dt))

        def sem(name):
            return ctx.enter_context(nc.semaphore(name))

        ps = ctx.enter_context(nc.psum_tensor("ps", [P, 8, T], F32))
        ring = sb("ring", [P, RING, UNIT])
        par = sb("par", [P, N_PAR])
        cst = sb("cst", [P, N_CST])
        ones = cst[:, 0:P]
        x = sb("x", [P, DC, T])
        rstd = sb("rstd", [P, T])

        identb = sb("identb", [P, P], BF16)
        causalb = sb("causalb", [P, P], BF16)
        cmpb = sb("cmpb", [P, TT, N_CMP], BF16)

        iota = sb("iota", [P, N_KEYS, GB], BF16)
        hns = ExitStack()
        hn = sb("hn", [P, DC, T], c=hns)
        both = ExitStack()
        rope = sb("rope", [P, 4, T], c=both)
        sq = sb("sq", [P, DC, T], c=both)

        one = ExitStack()
        merged = sb("merged", [P, DC, T], c=one)
        pw = merged
        pT = sb("pT", [P, 2, T], c=one)
        posi = sb("posi", [P, T], mybir.dt.int32, c=one)
        ang = sb("ang", [P, 3, T], c=one)
        sp = sb("sp", [P, 6, DC], c=one)
        rg = ExitStack()
        rxp = sb("rxp", [P, 2, 3 + T], c=rg)
        prod = sb("prod", [P, 2, 2 + T], c=rg)
        zb = {n: sb(f"z_{n}", [P, 2, T], c=rg) for n in ("ry", "cb", "cc", "cx", "gr", "gc")}
        xc = sb("xc", [P, 2, T], c=rg)
        r_g = sb("r_g", [P, 2, T], c=rg)
        i_g = sb("i_g", [P, 2, T], c=rg)
        a_t = sb("a_t", [P, 2, T], c=rg)
        th = sb("th", [P, 2, T], c=rg)
        mlt = sb("mlt", [P, 2, T], c=rg)
        hs = sb("hs", [P, 2, T], c=rg)
        rg.close()
        act = sb("act", [P, FC, T], c=one)
        sg = sb("sg", [P, 2, T], c=one)
        gate = sb("gate", [P, 2, T], c=one)
        one.close()

        two = ExitStack()
        qk = sb("qk", [P, A_R + 2, T], c=two)
        kcn = sb("kcn", [P, 1, A_G * N_CMP], c=two)
        vct = sb("vct", [N_CMP, A_G, A_D], c=two)
        vtok = sb("vtok", [P, TT, VW], c=two)
        mqk = sb("mqk", [B_QK, 2 * B_H, T], c=two)
        vm = sb("vm", [P, TT, B_H * B_V], c=two)
        pre = ExitStack()
        kcd = sb("kcd", [P, 4, T], c=pre)
        blk = sb("blk", [P, 2, CMP_LEN // 2, A_G * N_CMP], c=pre)
        hid = sb("hid", [P, 2, 2, A_G * N_CMP], c=pre)
        cq = sb("cq", [P, 3, T], c=pre)
        kr = sb("kr", [P, T], c=pre)
        sqt = sb("sqt", [P, 2, T], c=pre)
        rst = sb("rst", [P, 2, T], c=pre)
        xn = sb("xn", [P, 2, T], c=pre)
        rt = sb("rt", [P, 2, T], c=pre)
        pre.close()
        q_cur = sb("q_cur", [P, 2, T], c=two)
        k_cur = sb("k_cur", [P, 2, T], c=two)
        v_cur = sb("v_cur", [P, 2, TT, B_V], c=two)
        pr = sb("pr", [P, 3, T], c=two)
        pt = sb("pt", [P, 2, TT, T], c=two)
        st = sb("st", [P, 3, 4], c=two)
        oall = hn
        two.close()
        both.close()

        hns.close()
        ex = ExitStack()
        spl = sb("spl", [P, 2, 2, D], F32R, c=ex)
        hh = sb("hh", [P, DC, T], F32R, c=ex)
        hl = sb("hl", [P, DC, T], F32R, c=ex)
        ch = ExitStack()
        qp = sb("qp", [P, 2 * E_H, T], c=ch)
        fill = sb("fill", [P, EARLY - 16, T], c=ch)
        s_sb = sb("s_sb", [P, TT, 2 * E_H, N_KEYS], c=ch)
        ssq = sb("ssq", [P, 2, TT * E_H], c=ch)
        qs_mem = ExitStack()
        qs = sb("qs", [P, 4, T], c=qs_mem)
        qs_mem.close()
        tk = sb("tk", [P, 256], c=ch)
        cand = sb("cand", [P, E_K, E_K], c=ch)
        tv = sb("tv", [P, 2, E_H, E_K], c=ch)
        ti = sb("ti", [P, 2, E_H, E_K], mybir.dt.uint32, c=ch)
        tif = sb("tif", [P, 2, E_H, E_K], c=ch)
        cv = sb("cv", [P, E_H, E_K], c=ch)
        ci = sb("ci", [P, E_H, E_K], mybir.dt.uint32, c=ch)
        cm = sb("cm", [P, 2, E_H, E_K], mybir.dt.uint32, c=ch)
        cmf = sb("cmf", [P, 2, E_H, E_K], c=ch)
        ce = sb("ce", [P, E_H, E_K], c=ch)
        oh = sb("oh", [P, E_H, E_K, E_K], c=ch)
        sel = sb("sel", [P, TT, 3, E_H * E_K], c=ch)
        gs = sb("gs", [P, 2, E_H], c=ch)
        ch.close()
        gb = sb("gb", [P, QN, T], c=ex)
        wsp = sb("wsp", [P, 2, 2, 2 * T], F32R, c=ex)
        oh1 = sb("oh1", [P, 2, N_KEYS, GB], BF16, c=ex)
        oh2 = sb("oh2", [P, 2, 4, QN, GB], BF16, c=ex)
        n1t = sb("n1t", [P, T], BF16, c=ex)
        n2q = sb("n2q", [P, T], BF16, c=ex)
        g3 = sb("g3", [P, 3, T], BF16, c=ex)
        gf = sb("gf", [P, 2, T], c=ex)
        ex.close()

        in_evac, tok_evac, blk_ready, hid_ready = sem("in_evac"), sem("tok_evac"), sem("blk_ready"), sem("hid_ready")
        kc_evac, m_done, m_evac, mv_evac = sem("kc_evac"), sem("m_done"), sem("m_evac"), sem("mv_evac")
        rope_ang, rope_ready = sem("rope_ang"), sem("rope_ready")
        rsq, rss, rrms, rxn, rrot, rdone = (sem(f"rope_{v}") for v in ("sq", "ss", "rms", "xn", "rot", "done"))
        cur_ready = sem("cur_ready")
        at_s, at_max, at_exp, at_scale, at_t, at_ev, at_pv, at_out = (
            sem(f"at_{v}") for v in ("scores", "max", "exp", "scale", "transposed", "evacuated", "pv", "out"))
        qp_evac, ssq_done, ssq_sqrt, sk_done, sk_evac, rs_ready = (
            sem(v) for v in ("qp_evac", "ssq_done", "ssq_sqrt", "sk_done", "sk_evac", "rs_ready"))
        tk_sub, tk_exp, sel_ready, selt_done = (sem(v) for v in ("tk_sub", "tk_exp", "sel_ready", "selt_done"))
        oh_eq, n2_next = sem("oh_eq"), sem("n2_next")
        iota_ready, oh_ready, gx_done, gx_evac = (sem(v) for v in ("iota_ready", "oh_ready", "gx_done", "gx_evac"))
        hi_done, lo_done, e_done, hh_ready, hl_ready, hn_used = (sem(v) for v in ("hi_done", "lo_done", "e_done", "hh_ready", "hl_ready", "hn_used"))
        wh_ready, wl_ready, qs_used, ssq_sum = (sem(v) for v in ("wh_ready", "wl_ready", "qs_used", "ssq_sum"))
        gelu_done, y_add = sem("gelu_done"), sem("y_add")
        w_ready = [sem(f"w_ready{s}") for s in range(RING)]
        unit_done = sem("unit_done")
        loaded = sem("loaded")
        act_order, dve_order = sem("act_order"), sem("dve_order")
        sq_ready, ss_ready, rms_ready, hn_ready = sem("sq_ready"), sem("ss_ready"), sem("rms_ready"), sem("hn_ready")
        z_evac, xc_ready, rg_ready, rg_evac = sem("z_evac"), sem("xc_ready"), sem("rg_ready"), sem("rg_evac")
        th_ready, m2_ready, mlt_ready, a_ready = sem("th_ready"), sem("m2_ready"), sem("mlt_ready"), sem("a_ready")
        chunk_done, sp_exp, sp_ready, sp_abs = sem("chunk_done"), sem("sp_exp"), sem("sp_ready"), sem("sp_abs")
        silu_done, ff_act = sem("silu_done"), sem("ff_act")
        x_add = sem("x_add")
        ple_evac, gate_done = sem("ple_evac"), sem("gate_done")
        out_done = sem("out_done")

        def pc(name, n=1, at=0):
            return par[:, PAR[name] + at:PAR[name] + at + n]

        def cc(name, rows=P):
            a, b = CST[name]
            return cst[0:rows, a:b]

        NSA = [(g, b, qt) for g in range(A_G) for b in ("cmp", "slc", "win") for qt in range(TT)]
        MLA = [(h, "mla", qt) for h in range(2) for qt in range(TT)]

        def pd(name, idx):
            return par[:, bass.ds(idx + PAR[name], 1)]

        block = ctx.enter_context(nc.Block())

        @block.sync
        def _(sp_):
            sp_.dma_start(x[:, :, :], xT_in).then_inc(loaded, 16)
            sp_.dma_start(par[:, :], par_in).then_inc(loaded, 16)
            sp_.dma_start(cst[:, :], cst_in).then_inc(loaded, 16)
            for s in range(RING):
                sp_.dma_start(ring[:, s, :], stream[s, :, :]).then_inc(w_ready[s], 16)
            sp_.dma_start(pT[:, :, :], pT_in).then_inc(loaded, 16)
            sp_.dma_start(posi[:, :], pos_in).then_inc(loaded, 16)
            with sp_.Fori(0, N_UNITS // RING - 1) as i:
                for s in range(RING):
                    sp_.wait_ge(unit_done, i * RING + (s + 1))
                    sp_.dma_start(ring[:, s, :], stream[bass.ds(i * RING + (RING + s), 1), :, :]
                                  .rearrange("a p n -> p (a n)")).then_inc(w_ready[s], 16)
            for u in range(N_UNITS // RING * RING, N_UNITS):
                sp_.wait_ge(unit_done, u - RING + 1)
                sp_.dma_start(ring[:, u % RING, :], stream[u, :, :]).then_inc(w_ready[u % RING], 16)
            sp_.wait_ge(unit_done, U_EXP)
            sp_.sem_inc(lo_done, RING)
            with sp_.Fori(0, NQ) as q:
                for first, count, src, half in ((0, E_A, u_in, 0), (E_A, E_Y, v_in, 0), (E_A + E_Y, E_Y, v_in, 1)):
                    with sp_.Fori(0, count // RING) as i:
                        for j in range(RING):
                            sp_.wait_ge(lo_done, q * E_Q + i * RING + (first + j + 1))
                            if src is u_in:
                                unit = u_in[bass.ds(q * E_A + i * RING + j, 1), :, :]
                            else:
                                unit = v_in[bass.ds(q * (2 * E_Y) + i * RING + (half * E_Y + j), 1), :, :]
                            sp_.dma_start(ring[:, j, 0:D], unit.rearrange("a p n -> p (a n)")).then_inc(w_ready[j], 16)
            sp_.wait_ge(y_add, HB + NQ * DC)
            sp_.dma_start(out, x[:, :, :]).then_inc(out_done, 16)
            sp_.wait_ge(out_done, 16)

        @block.tensor
        def _(pe):
            def need(u, i=None, per=0):
                v = 16 * (u // RING + 1)
                pe.wait_ge(w_ready[u % RING], v if i is None else i * (16 * per // RING) + v)
                return ring[:, u % RING, :]

            def chunk(bank, w, rhs, k0=0, start=True, stop=True, kn=None):
                kn = rhs.shape[1] if kn is None else kn
                for k in range(kn):
                    m = pe.matmul(ps[:, bank, :], w[:, k * P:(k + 1) * P], rhs[:, k0 + k, :],
                                  start=start and k == 0, stop=stop and k == kn - 1)
                return m

            def norm(n):
                for c in range(NORMS[n]):
                    pe.wait_ge(sq_ready, NB[n] + c + 1)
                    m = pe.matmul(ps[:, 7, :], ones, sq[:, c, :], start=c == 0, stop=c == NORMS[n] - 1)
                m.then_inc(ss_ready, 1)

            def residual(u, passes, units):
                rhs = {U_OUT: merged, U_DOWN: act, U_OUT2: oall}[u]
                with pe.Fori(0, passes) as i:
                    for j in range(4 // units):
                        pe.wait_ge(x_add, i * (4 // units) + (X_BASE[u] + j + 1))
                        for h in range(units):
                            w = need(u + j * units + h, i, 4)
                            n = DC if units == 1 else FC // 2
                            chunk(3 + j, w, rhs, k0=h * (FC // 2), kn=n, start=h == 0, stop=h == units - 1)\
                                .then_inc(unit_done, 1)

            pe.wait_ge(loaded, 80)
            norm(0)
            pe.wait_ge(hn_ready, DC)
            with pe.Fori(0, HEADS_RG) as i:
                for k, (name, a) in enumerate(Z_ORDER):
                    if k == 6:
                        pe.wait_ge(xc_ready, i * 2 + 2)
                        for g in range(2):
                            w = need(RG_UNIT + g, i, 16)
                            for o in range(2):
                                pe.wait_ge(rg_evac, i * 4 + (2 * g + o + 1))
                                for kk in range(2):
                                    m = pe.matmul(ps[:, 7, :], w[:, (2 * kk + o) * P:(2 * kk + o + 1) * P],
                                                  xc[:, kk, :], start=kk == 0, stop=kk == 1)
                                m.then_inc(unit_done if o else rg_ready, 1)
                    w = need(Z_UNIT[k], i, 16)
                    pe.wait_ge(z_evac, i * 14 + (k + 1))
                    chunk(k % Z_BANKS, w, hn).then_inc(unit_done, 1)
            pe.wait_ge(chunk_done, 2 + DC)
            residual(U_OUT, 2, 1)
            norm(1)
            pe.wait_ge(hn_ready, 2 * DC)
            with pe.Fori(0, FC // 2) as i:
                for j in range(2):
                    w = need(U_FF + 2 * j, i, 4)
                    pe.wait_ge(silu_done, i * 2 + (j + 1))
                    chunk(2 * j, w, hn).then_inc(unit_done, 1)
                    w = need(U_FF + 2 * j + 1, i, 4)
                    pe.wait_ge(ff_act, i * 2 + (j + 1))
                    chunk(2 * j + 1, w, hn).then_inc(unit_done, 1)
            for g in range(2):
                if g == 0:
                    pe.wait_ge(ff_act, 2 + FC)
            residual(U_DOWN, 4, 2)
            pe.wait_ge(silu_done, 2 + FC)
            pe.wait_ge(x_add, X_BASE[U_GATE])
            for g in range(2):
                w = need(U_PLE + g)
                for j in range(4):
                    if g:
                        pe.wait_ge(ple_evac, j + 1)
                    for kk in range(2):
                        m = pe.matmul(ps[:, j, :], w[:, (2 * j + kk) * P:(2 * j + kk + 1) * P], pT[:, kk, :],
                                      start=kk == 0, stop=kk == 1)
                m.then_inc(unit_done, 1)
            norm(2)
            pe.wait_ge(hn_ready, 3 * DC)
            for c in range(DC):
                w = need(U_GATE + c)
                if c < 4:
                    pe.wait_ge(ple_evac, 5 + c)
                else:
                    pe.wait_ge(gate_done, c - 3)
                chunk(c % 4, w, hn).then_inc(unit_done, 1)
            norm(3)
            norm(4)
            pe.wait_ge(hn_ready, NB[5])
            for c in range(14):
                w = need(U_IN2 + c)
                if c >= 4:
                    pe.wait_ge(in_evac, c - 3)
                chunk(c % 4, w, hn).then_inc(unit_done, 1)
            for h in range(2):
                w = need(U_TOK + h)
                for t in range(TT):
                    for k in range(4):
                        m = pe.matmul(ps[:, 4 + t, 0:VW], hn[:, 4 * h + k, t * P:(t + 1) * P], w[:, k * VW:(k + 1) * VW],
                                      start=h == 0 and k == 0, stop=h == 1 and k == 3)
                m.then_inc(unit_done, 1)
            pe.wait_ge(in_evac, 14)
            for kv in range(2):
                pe.wait_ge(blk_ready, kv + 1)
                for m_ in range(2):
                    for h in range(2):
                        w = need(U_CMP + kv * 4 + m_ * 2 + h)
                        for j in range(8):
                            m = pe.matmul(ps[:, kv * 2 + m_, 0:A_G * N_CMP], w[:, j * P:(j + 1) * P],
                                          blk[:, kv, 8 * h + j, :], start=h == 0 and j == 0, stop=h == 1 and j == 7)
                        m.then_inc(unit_done, 1)
            w = need(U_CMP2)
            pe.wait_ge(tok_evac, 2 * TT)
            pe.wait_ge(hid_ready, 4)
            for m_ in range(2):
                pe.matmul(ps[:, 4, 0:A_G * N_CMP], w[:, m_ * P:(m_ + 1) * P], hid[:, 0, m_, :], start=m_ == 0, stop=m_ == 1)
            for g in range(A_G):
                for m_ in range(2):
                    m = pe.matmul(ps[0:N_CMP, 5, g * A_D:(g + 1) * A_D], hid[:, 1, m_, g * N_CMP:(g + 1) * N_CMP],
                                  w[:, 2 * P + m_ * A_D:2 * P + (m_ + 1) * A_D], start=m_ == 0, stop=m_ == 1)
            m.then_inc(unit_done, 1)
            norm(5)
            norm(6)
            pe.wait_ge(hn_ready, NB[7])
            for h in range(B_H):
                w = need(U_UQ + h // 4)
                if h >= 4:
                    pe.wait_ge(m_evac, h - 3)
                for k in range(2):
                    m = pe.matmul(ps[0:B_QK, h % 4, :], w[:, (k * 4 + h % 4) * B_QK:(k * 4 + h % 4 + 1) * B_QK], cq[:, k, :],
                                  start=k == 0, stop=k == 1)
                m.then_inc(unit_done if h % 4 == 3 else m_done, 1)
            w = need(U_UKV)
            for h in range(B_H):
                pe.wait_ge(m_evac, 5 + h)
                pe.matmul(ps[0:B_NOPE, h % 4, :], w[:, h * B_NOPE:(h + 1) * B_NOPE], cq[:, 2, :],
                          start=True, stop=True).then_inc(m_done, 1)
            pe.wait_ge(kc_evac, 2)
            for t in range(TT):
                if t >= 2:
                    pe.wait_ge(mv_evac, t - 1)
                m = pe.matmul(ps[:, 4 + t % 2, :], cq[:, 2, t * P:(t + 1) * P], w[:, 512:1024], start=True, stop=True)
                m.then_inc(unit_done if t == 3 else m_done, 1)
            pe.wait_ge(m_evac, 2 * B_H)

            def rope_items(i, base, per, rows, blk_c, rot_c, cols=T):
                n = [(i * 2 if i is not None else 0) + (base + j + 1) for j in range(per)]
                for j in range(per):
                    pe.wait_ge(rsq, n[j])
                    pe.matmul(ps[0:rows, j, 0:cols], blk_c, sqt[0:rows, j, 0:cols], start=True, stop=True).then_inc(rss, 1)
                for j in range(per):
                    pe.wait_ge(rxn, n[j])
                    pe.matmul(ps[0:rows, 2 + j, 0:cols], rot_c, xn[0:rows, j, 0:cols], start=True, stop=True).then_inc(rrot, 1)

            with pe.Fori(0, 3) as i:
                rope_items(i, 0, 2, P, cc("blk"), cc("rot_a"))
            rope_items(None, 6, 1, P, cc("blk"), cc("rot_a"), A_G * N_CMP)
            with pe.Fori(0, B_H) as i:
                rope_items(i, 7, 2, B_QK, cst[0:B_QK, 0:B_QK], cc("rot_b", B_QK))

            def attend(i, units, base):
                per = len(units)
                for s in range(per + 2):
                    if s < per:
                        g, kind, qt = units[s]
                        if s >= 3:
                            pe.wait_ge(at_exp, i * per + (base + s - 2))
                        bank, lo = s % 3, A_D * g
                        if kind == "mla":
                            nk = (qt + 1) * P
                            pe.matmul(ps[:, bank, 0:nk], q_cur[0:B_QK, g, qt * P:(qt + 1) * P], k_cur[0:B_QK, g, 0:nk],
                                      start=True, stop=False)
                        elif kind == "cmp":
                            nk = N_CMP
                            pe.matmul(ps[:, bank, 0:nk], q_cur[lo:lo + A_D, 0, qt * P:(qt + 1) * P],
                                      kcn[lo:lo + A_D, 0, g * N_CMP:(g + 1) * N_CMP], start=True, stop=False)
                        else:
                            nk = (qt + 1) * P
                            pe.matmul(ps[:, bank, 0:nk], q_cur[lo:lo + A_D, 0, qt * P:(qt + 1) * P],
                                      qk[lo:lo + A_D, A_R + (kind == "win"), 0:nk], start=True, stop=False)
                        if kind == "cmp":
                            m = pe.matmul(ps[:, bank, 0:nk], identb[:, :], cmpb[:, qt, :], start=False, stop=True)
                        else:
                            m = pe.matmul(ps[:, bank, nk - P:nk], identb[:, :], causalb[:, :], start=False, stop=True)
                        m.then_inc(at_s, 1)
                    if s >= 2:
                        u = s - 2
                        g, kind, qt = units[u]
                        pe.wait_ge(at_scale, i * per + (base + u + 1))
                        if u >= 2:
                            pe.wait_ge(at_ev, i * per + (base + u - 1))
                        if kind == "cmp":
                            m = pe.transpose(ps[0:N_CMP, 3 + u % 2, 0:P], pr[:, u % 3, 0:N_CMP], cc("ident"))
                        else:
                            for kt in range(qt + 1):
                                m = pe.transpose(ps[:, 3 + u % 2, kt * P:(kt + 1) * P], pr[:, u % 3, kt * P:(kt + 1) * P],
                                                 cc("ident"))
                        m.then_inc(at_t, 1)
                    if s >= 3 and (s - 3) % TT == TT - 1:
                        output(i, units, s - 3, base)
                output(i, units, per - 1, base)

            def output(i, units, u, base):
                per = len(units)
                g, kind, _ = units[u]
                grp = u // TT
                pe.wait_ge(at_ev, i * per + (base + u + 1))
                lo = A_D * g
                first = kind in ("cmp", "mla")
                if kind == "cmp":
                    m = pe.matmul(ps[lo:lo + A_D, 5, :], vct[:, g, :], pt[0:N_CMP, grp % 2, 0, :], start=True, stop=False)
                else:
                    for kt in range(TT):
                        if kind == "mla":
                            v = v_cur[:, g, kt, :]
                        else:
                            c = (kind == "win") * P + lo
                            v = vtok[:, kt, c:c + A_D]
                        m = pe.matmul(ps[lo:lo + A_D, 5, kt * P:], v, pt[:, grp % 2, kt, kt * P:],
                                      start=first and kt == 0, stop=kt == TT - 1 and kind != "slc")
                m.then_inc(at_pv, 1)

            pe.wait_ge(rdone, 2 + 7 + 2 * B_H)
            with pe.Fori(0, A_R) as i:
                pe.wait_ge(cur_ready, i + 1)
                pe.wait_ge(at_out, i + 1)
                attend(i, NSA, S_NSA)
            with pe.Fori(0, B_H // 2) as i:
                pe.wait_ge(cur_ready, i * 6 + (A_R + 6))
                pe.wait_ge(at_out, i + (A_R + 1))
                attend(i, MLA, S_MLA)
            norm(7)
            norm(8)
            pe.wait_ge(hn_ready, NB[9])
            residual(U_OUT2, 2, 1)
            norm(9)
            pe.wait_ge(hn_ready, NB[10])
            for c in range(2 * E_H + 1):
                if c < 2 * E_H:
                    w = need(U_WQ + c)
                    if c >= 4:
                        pe.wait_ge(qp_evac, 2 * (c - 3))
                    chunk(c % 4, w, hn).then_inc(unit_done, 1)
                if c:
                    pe.wait_ge(qp_evac, 2 * c)
                    for t in range(TT):
                        col = (c - 1) % 2 * TT * E_H + t * E_H + (c - 1) // 2
                        m = pe.matmul(ps[:, 6, col:col + 1], qs[:, (c - 1) % 4, t * P:(t + 1) * P], ones[:, 0:1],
                                      start=True, stop=True)
                    m.then_inc(qs_used, 1)
            need(U_KEYS)
            need(U_KEYS + 1)
            n = 0
            for t in range(TT):
                for b in range(4):
                    if n >= 4:
                        pe.wait_ge(sk_evac, 2 * (n - 3))
                    for j in range(4):
                        c = 4 * b + j
                        m = pe.matmul(ps[:, n % 4, j * P:(j + 1) * P], qp[:, c, t * P:(t + 1) * P],
                                      ring[:, (U_KEYS + c // 8) % RING, (c % 8) * P:(c % 8 + 1) * P], start=True, stop=True)
                    m.then_inc(sk_done, 1)
                    n += 1
            pe.wait_ge(sk_evac, 32)
            pe.sem_inc(unit_done, 2)
            pe.sem_inc(hn_used, 1)
            def split_products(bank, w, k0, kn, n, high, low, first, last):
                for k in range(kn):
                    for part, rhs in ((0, high), (0, low), (1, high)):
                        m = pe.matmul(ps[:, bank, :], w[:, part, k0 + k * n:k0 + k * n + P], rhs(k),
                                      start=first and k == 0 and part == 0 and rhs is high,
                                      stop=last and k == kn - 1 and part == 1)
                return m

            def experts_in(q):
                with pe.Fori(0, E_A // 4) as i:
                    for j in range(4):
                        pe.wait_ge(lo_done, q * E_Q + i * 4 + (RING + j + 1))
                        pe.wait_ge(gelu_done, q * E_A + i * 4 + (j + 1))
                        split_products(j, spl[:, j % 2, :, :], 0, DC, P, lambda k: hh[:, k, :], lambda k: hl[:, k, :],
                                       True, True).then_inc(e_done, 1)

            def spread(q):
                with pe.Fori(0, T // GB // 2) as b:
                    for j in range(2):
                        pe.wait_ge(oh_ready, q * (T // GB) + b * 2 + (j + 1))
                        pe.wait_ge(gx_evac, q * (T // GB) + b * 2 + (j + 1))
                        for t in range(GB):
                            for k in range(3):
                                m = pe.matmul(ps[:, 4 + j, t * QN:(t + 1) * QN], oh1[:, j, :, t], oh2[:, j, 1 + k, :, t],
                                              start=k == 0, stop=k == 2)
                        m.then_inc(gx_done, 1)

            def experts_out(q):
                for half in range(2):
                    def unit(i, j, first, last):
                        e = q * E_Q + i * 4 + (E_A + half * E_Y + j)
                        pe.wait_ge(lo_done, e + (RING + 1))
                        pe.wait_ge(wl_ready, q * (2 * E_Y) + i * 4 + (half * E_Y + j + 1))
                        for k in range(2):
                            for c in range(HB):
                                m = split_products(4 + c, spl[:, j % 2, :, :], k * HB * P + c * P, 1, P,
                                                   lambda _: wsp[:, j % 2, 0, k * T:(k + 1) * T],
                                                   lambda _: wsp[:, j % 2, 1, k * T:(k + 1) * T],
                                                   first and k == 0, last and k == 1)
                        m.then_inc(e_done, 1)
                    pe.wait_ge(gx_evac, q * (T // GB) + (T // GB + 2)) if half == 0 else None
                    pe.wait_ge(y_add, q * DC + (half * HB + HB))
                    for j in range(4):
                        unit(0, j, j == 0, False)
                    with pe.Fori(1, E_Y // 4 - 1) as i:
                        for j in range(4):
                            unit(i, j, False, False)
                    for j in range(4):
                        unit(E_Y // 4 - 1, j, False, j == 3)

            pe.wait_ge(hl_ready, DC)
            experts_in(0)
            for t in range(TT):
                pe.wait_ge(sel_ready, t + 1)
                for k in range(3):
                    m = pe.transpose(ps[:, 4 + k, t * P:(t + 1) * P], sel[:, t, k, :], cc("ident"))
            m.then_inc(selt_done, 1)
            spread(0)
            experts_out(0)
            with pe.Fori(1, NQ) as q:
                experts_in(q)
                spread(q)
                experts_out(q)

        @block.scalar
        def _(eng):
            def squares(n, wait=None, src=x, at=0):
                for c in range(NORMS[n]):
                    if wait is not None:
                        eng.wait_ge(wait[0], wait[1] + c + 1)
                    if n:
                        eng.wait_ge(ss_ready, n)
                    eng.activation(sq[:, c, :], src[:, at + c, :], ACT.Square).then_inc(sq_ready, 1)

            def rms(n, width=D):
                eng.wait_ge(ss_ready, n + 1)
                if n:
                    eng.wait_ge(hn_ready, NB[n])
                eng.activation(rstd[:, :], ps[:, 7, :], ACT.Sqrt, scale=1.0 / width, bias=pc("eps")).then_inc(rms_ready, 1)

            eng.wait_ge(loaded, 80)
            squares(0)
            eng.wait_ge(sp_abs, 1)
            eng.activation(sp[:, 1, :], sp[:, 0, :], ACT.Exp, scale=-1.0).then_inc(sp_exp, 1)
            rms(0)
            eng.sem_inc(z_evac, Z_BANKS)
            eng.sem_inc(rg_evac, 1)
            eng.wait_ge(sp_ready, 2)

            def z(i, k, func, dst, **kw):
                eng.wait_ge(unit_done, i * 16 + (Z_UNIT[k] + 1))
                eng.activation(dst, ps[:, k % Z_BANKS, :], func, **kw).then_inc(z_evac, 1)

            with eng.Fori(0, HEADS_RG) as i:
                for k, (name, a) in enumerate(Z_ORDER):
                    if k == 6:
                        for g, (dst, b) in enumerate(((r_g, "b_r"), (i_g, "b_i"))):
                            for o in range(2):
                                if o:
                                    eng.wait_ge(unit_done, i * 16 + (RG_UNIT + g + 1))
                                else:
                                    eng.wait_ge(rg_ready, i * 2 + (g + 1))
                                eng.activation(dst[:, o, :], ps[:, 7, :], ACT.Sigmoid, bias=pd(b, i * 2 + o))\
                                    .then_inc(rg_evac, 1)
                        eng.wait_ge(rg_evac, i * 4 + 5)
                        for o in range(2):
                            eng.activation(th[:, o, :], r_g[:, o, :], ACT.Tanh, scale=sp[:, 4, bass.ds(i * 2 + o, 1)])\
                                .then_inc(th_ready, 1)
                        for o in range(2):
                            eng.activation(a_t[:, o, :], r_g[:, o, :], ACT.Exp, scale=sp[:, 5, bass.ds(i * 2 + o, 1)])\
                                .then_inc(a_ready, 1)
                        for o in range(2):
                            eng.wait_ge(m2_ready, i * 2 + (o + 1))
                            eng.activation(mlt[:, o, :], mlt[:, o, :], ACT.Sqrt, scale=2.0).then_inc(mlt_ready, 1)
                    if k < 2:
                        eng.wait_ge(chunk_done, i * 2 + (k + 1))
                        z(i, k, ACT.Copy, rxp[:, k, 3:])
                    elif name == "ry":
                        z(i, k, ACT.Gelu_apprx_tanh, zb["ry"][:, a, :])
                    elif name in ("gr", "gc"):
                        z(i, k, ACT.Sigmoid, zb[name][:, a, :])
                    else:
                        z(i, k, ACT.Copy, zb[name][:, a, :])
            eng.sem_inc(silu_done, 2)
            squares(1, (x_add, X_BASE[U_OUT] + 4))
            rms(1)
            for k in range(4):
                eng.wait_ge(rope_ang, k + 1)
                eng.activation(rope[:, k, :], rope[:, k, :], ACT.Sin).then_inc(rope_ready, 1)
            with eng.Fori(0, FC // 2) as i:
                for j in range(2):
                    eng.wait_ge(unit_done, i * 4 + (U_FF + 2 * j + 1))
                    eng.wait_ge(ff_act, i * 2 + (j + 1))
                    eng.activation(sg[:, j, :], ps[:, 2 * j, :], ACT.Silu).then_inc(silu_done, 1)
            squares(2, (x_add, X_BASE[U_DOWN] + 2))
            for g in range(2):
                eng.wait_ge(unit_done, U_PLE + g + 1)
                for j in range(4):
                    eng.activation(pw[:, 4 * g + j, :], ps[:, j, :], ACT.Copy).then_inc(ple_evac, 1)
            rms(2)
            for c in range(DC):
                eng.wait_ge(unit_done, U_GATE + c + 1)
                if c >= 2:
                    eng.wait_ge(x_add, X_BASE[U_GATE] + c - 1)
                eng.activation(gate[:, c % 2, :], ps[:, c % 4, :], ACT.Sigmoid).then_inc(gate_done, 1)
            squares(3, (x_add, X_BASE[U_GATE]))
            rms(3)
            squares(4, (hn_ready, NB[3]))
            rms(4)
            for c in range(14):
                eng.wait_ge(unit_done, U_IN2 + c + 1)
                b = ps[:, c % 4, :]
                if c < 4 or c in (8, 9):
                    eng.activation(qk[:, c if c < 4 else c - 4, :], b, ACT.Copy).then_inc(in_evac, 1)
                elif c < 8:
                    eng.activation(kcd[0:A_D, c - 4, :], b[0:A_D, :], ACT.Copy)
                    eng.activation(kcd[A_D:, c - 4, 0:T - 1], b[A_D:, 1:T], ACT.Copy).then_inc(in_evac, 1)
                elif c < 13:
                    eng.activation(cq[:, c - 10, :], b, ACT.Copy).then_inc(in_evac, 1)
                else:
                    eng.activation(kr[B_NOPE:B_QK, :], b[B_NOPE:B_QK, :], ACT.Copy).then_inc(in_evac, 1)
            eng.wait_ge(unit_done, U_TOK + 2)
            for t in range(TT):
                eng.activation(vtok[:, t, 0:2 * P], ps[:, 4 + t, 0:2 * P], ACT.Copy).then_inc(tok_evac, 1)
            for t in range(TT):
                eng.activation(vtok[:, t, 2 * P:VW], ps[:, 4 + t, 2 * P:VW], ACT.Sigmoid).then_inc(tok_evac, 1)
            for kv in range(2):
                for m in range(2):
                    eng.wait_ge(unit_done, U_CMP + kv * 4 + m * 2 + 2)
                    eng.activation(hid[:, kv, m, :], ps[:, kv * 2 + m, 0:A_G * N_CMP], ACT.Gelu_apprx_tanh)\
                        .then_inc(hid_ready, 1)
            eng.wait_ge(unit_done, U_CMP2 + 1)
            eng.activation(kcn[:, 0, :], ps[:, 4, 0:A_G * N_CMP], ACT.Copy).then_inc(kc_evac, 1)
            eng.activation(vct[:, :, :].rearrange("p a d -> p (a d)"), ps[0:N_CMP, 5, 0:A_G * A_D], ACT.Copy)\
                .then_inc(kc_evac, 1)
            eng.wait_ge(in_evac, 14)
            squares(5, src=cq)
            rms(5, Q_LORA)
            squares(6, src=cq, at=2)
            rms(6, P)
            for h in range(B_H):
                if h % 4 == 3:
                    eng.wait_ge(unit_done, U_UQ + h // 4 + 1)
                else:
                    eng.wait_ge(m_done, h - h // 4 + 1)
                eng.activation(mqk[:, h, :], ps[0:B_QK, h % 4, :], ACT.Copy).then_inc(m_evac, 1)
            for h in range(B_H):
                eng.wait_ge(m_done, 6 + h + 1)
                eng.activation(mqk[0:B_NOPE, B_H + h, :], ps[0:B_NOPE, h % 4, :], ACT.Copy).then_inc(m_evac, 1)
            for t in range(TT):
                if t == 3:
                    eng.wait_ge(unit_done, U_UKV + 1)
                else:
                    eng.wait_ge(m_done, 14 + t + 1)
                eng.activation(vm[:, t, :], ps[:, 4 + t % 2, :], ACT.Copy).then_inc(mv_evac, 1)

            def rope_items(i, base, per, rows, src, width, cols=T):
                n = [(i * 2 if i is not None else 0) + (base + j + 1) for j in range(per)]
                for j in range(per):
                    at = bass.ds(i * 2 + j, 1) if i is not None else slice(0, 1)
                    eng.activation(sqt[0:rows, j, 0:cols], src[0:rows, at, 0:cols].rearrange("p a t -> p (a t)"),
                                   ACT.Square).then_inc(rsq, 1)
                for j in range(per):
                    eng.wait_ge(rss, n[j])
                    eng.wait_ge(rdone, n[j])
                    eng.activation(rst[0:rows, j, 0:cols], ps[0:rows, j, 0:cols], ACT.Sqrt, scale=1.0 / width,
                                   bias=par[0:rows, PAR["eps"]:PAR["eps"] + 1]).then_inc(rrms, 1)

            eng.wait_ge(m_evac, 2 * B_H)
            with eng.Fori(0, 3) as i:
                rope_items(i, 0, 2, P, qk, A_D)
            rope_items(None, 6, 1, P, kcn, A_D, A_G * N_CMP)
            eng.wait_ge(rope_ready, 5)
            with eng.Fori(0, B_H) as i:
                rope_items(i, 7, 2, B_QK, mqk, B_QK)
            eng.sem_inc(at_out, 1)

            def attend(i, units, base, pvbase):
                per, groups = len(units), len(units) // TT
                for s in range(per + 2):
                    if s < per:
                        g, kind, qt = units[s]
                        nk = N_CMP if kind == "cmp" else (qt + 1) * P
                        eng.wait_ge(at_max, i * per + (base + s + 1))
                        if s >= 3:
                            eng.wait_ge(at_t, i * per + (base + s - 2))
                        eng.activation(pr[:, s % 3, 0:nk], ps[:, s % 3, 0:nk], ACT.Exp, bias=st[:, s % 3, 0:1],
                                       accum_out=st[:, s % 3, 1:2]).then_inc(at_exp, 1)
                    if s >= 2:
                        u = s - 2
                        g, kind, qt = units[u]
                        grp = u // TT
                        eng.wait_ge(at_t, i * per + (base + u + 1))
                        if grp >= 2:
                            eng.wait_ge(at_pv, i * groups + (pvbase + grp - 1))
                        if kind == "cmp":
                            eng.activation(pt[0:N_CMP, grp % 2, 0, qt * P:(qt + 1) * P], ps[0:N_CMP, 3 + u % 2, 0:P],
                                           ACT.Copy).then_inc(at_ev, 1)
                        else:
                            eng.activation(pt[:, grp % 2, 0:qt + 1, qt * P:(qt + 1) * P],
                                           ps[:, 3 + u % 2, 0:(qt + 1) * P].rearrange("p (k q) -> p k q", q=P),
                                           ACT.Copy).then_inc(at_ev, 1)
                eng.wait_ge(at_pv, i * groups + (pvbase + groups))

            with eng.Fori(0, A_R) as i:
                attend(i, NSA, S_NSA, 0)
                eng.activation(oall[:, bass.ds(i, 1), :].rearrange("p a t -> p (a t)"), ps[:, 5, :], ACT.Copy)\
                    .then_inc(at_out, 1)
            with eng.Fori(0, B_H // 2) as i:
                attend(i, MLA, S_MLA, A_R * len(NSA) // TT)
                eng.activation(oall[:, bass.ds(i + A_R, 1), :].rearrange("p a t -> p (a t)"), ps[:, 5, :], ACT.Copy)\
                    .then_inc(at_out, 1)
            eng.wait_ge(at_out, 9)
            squares(7, src=oall)
            rms(7, A_H * A_D)
            squares(8, src=oall, at=4)
            rms(8, B_H * B_V)
            squares(9, (x_add, X_BASE[U_OUT2] + 4))
            rms(9)
            for c in range(DC):
                eng.wait_ge(hn_ready, NB[9] + c + 1)
                eng.activation(hh[:, c, :], hn[:, c, :], ACT.Copy).then_inc(hh_ready, 1)
            for c in range(2 * E_H):
                eng.wait_ge(unit_done, U_WQ + c + 1)
                eng.activation(qp[:, c, :], ps[:, c % 4, :], ACT.Copy).then_inc(qp_evac, 1)
                if c >= 4:
                    eng.wait_ge(qs_used, c - 3)
                eng.activation(qs[:, c % 4, :], ps[:, c % 4, :], ACT.Square).then_inc(qp_evac, 1)
            eng.wait_ge(ssq_sum, 1)
            eng.activation(ssq[:, 0, :], ssq[:, 0, :], ACT.Sqrt, scale=1.0 / (2 * N_KEYS), bias=pc("eps"))\
                .then_inc(ssq_sqrt, 1)
            eng.wait_ge(rs_ready, 1)
            n = 0
            for t in range(TT):
                for b in range(4):
                    eng.wait_ge(sk_done, n + 1)
                    for j in range(2):
                        h = 2 * b + j
                        eng.activation(s_sb[:, t, 2 * h:2 * h + 2, :].rearrange("p a n -> p (a n)"),
                                       ps[:, n % 4, j * 256:(j + 1) * 256], ACT.Copy,
                                       scale=ssq[:, 0, t * E_H + h:t * E_H + h + 1]).then_inc(sk_evac, 1)
                    n += 1
            eng.wait_ge(sk_evac, 2 * 4 * TT)
            eng.sem_inc(gelu_done, 4)

            def weights(t):
                eng.wait_ge(tk_sub, t + 1)
                eng.activation(ce[:, :, :], ce[:, :, :], ACT.Exp).then_inc(tk_exp, 1)

            def high(e, j):
                eng.wait_ge(w_ready[j % RING], e * (16 // RING) + (16 * (U_EXP // RING + 1) - j % RING * (16 // RING)))
                eng.wait_ge(e_done, e + 1)
                eng.activation(spl[:, j % 2, 0, :], ring[:, j % RING, 0:D], ACT.Copy).then_inc(hi_done, 1)

            def gelus(q, i0, i1):
                with eng.Fori(i0, i1) as i:
                    for j in range(4):
                        eng.wait_ge(e_done, q * E_Q + i * 4 + (2 + j + 1))
                        high(q * E_Q + i * 4 + (j + 2), j + 2)
                        eng.activation(gb[:, bass.ds(i * 4 + j, 1), :].rearrange("p a t -> p (a t)"), ps[:, j, :],
                                       ACT.Gelu_apprx_tanh).then_inc(gelu_done, 1)

            def w_high(at, j):
                eng.activation(wsp[:, j % 2, 0, :], gb[:, at, :].rearrange("p a t -> p (a t)"), ACT.Copy)\
                    .then_inc(wh_ready, 1)

            def outs(q, last):
                eng.wait_ge(gx_evac, q * (T // GB) + (T // GB + 2))
                w_high(slice(0, 2), 0)
                w_high(slice(2, 4), 1)
                for half in range(2):
                    e0 = E_A + half * E_Y
                    with eng.Fori(0, E_Y // 4 - 1) as i:
                        for j in range(4):
                            eng.wait_ge(e_done, q * E_Q + i * 4 + (e0 + 2 + j + 1))
                            high(q * E_Q + i * 4 + (e0 + j + 2), j + 2)
                            w_high(bass.ds(i * 8 + (2 * (j + 2)), 2), j)
                    for j in range(4):
                        e = q * E_Q + (e0 + E_Y - 4 + j)
                        eng.wait_ge(e_done, e + 3)
                        if not (last and half == 1 and j >= 2):
                            high(e + 2, j + 2)
                        if j < 2:
                            w_high(slice(QN - 4 + 2 * j, QN - 2 + 2 * j), j)
                        elif half == 0:
                            w_high(slice(2 * j - 4, 2 * j - 2), j)

            eng.wait_ge(hn_used, 1)
            eng.wait_ge(hl_ready, DC)
            eng.sem_inc(e_done, 2)
            for j in range(2):
                high(j, j)
            gelus(0, 0, 3)
            weights(0)
            gelus(0, 3, EARLY // 4)
            weights(1)
            eng.wait_ge(sel_ready, 2)
            gelus(0, EARLY // 4, E_A // 4)
            weights(2)
            weights(3)
            outs(0, False)
            with eng.Fori(1, NQ - 1) as q:
                gelus(q, 0, E_A // 4)
                outs(q, False)
            gelus(NQ - 1, 0, E_A // 4)
            outs(NQ - 1, True)

        @block.vector
        def _(dve):
            step = Order(dve, dve_order)

            def scale(n, g, dst, src=x, at=0, g_at=0):
                dve.wait_ge(rms_ready, n + 1)
                step(dve.reciprocal(rstd[:, :], rstd[:, :]))
                for c in range(NORMS[n]):
                    dve.scalar_tensor_tensor(out=dst[:, at + c, :], in0=src[:, at + c, :], scalar=pc(g, at=g_at + c),
                                             in1=rstd[:, :], op0=ALU.mult, op1=ALU.mult).then_inc(hn_ready, 1)

            def fma(dst, a, w, b):
                step(dve.scalar_tensor_tensor(out=dst, in0=a, scalar=w, in1=b, op0=ALU.mult, op1=ALU.add))

            dve.wait_ge(loaded, 80)
            lam = pc("lam", DC)
            step(dve.tensor_scalar(sp[:, 2, :], lam, -1.0, None, ALU.mult))
            dve.tensor_tensor(sp[:, 0, :], lam, sp[:, 2, :], ALU.max).then_inc(sp_abs, 1)
            step(dve.tensor_scalar(sp[:, 2, :], sp[:, 2, :], 0.0, None, ALU.max))
            dve.wait_ge(sp_exp, 1)
            step(dve.tensor_scalar(sp[:, 3, :], sp[:, 1, :], 2.0, None, ALU.add))
            step(dve.reciprocal(sp[:, 3, :], sp[:, 3, :]))
            step(dve.tensor_tensor(sp[:, 3, :], sp[:, 1, :], sp[:, 3, :], ALU.mult))
            step(dve.tensor_tensor(sp[:, 4, :], sp[:, 3, :], sp[:, 3, :], ALU.mult))
            step(dve.memset(sp[:, 5, :], 2.0 / 17))
            for n in (15, 13, 11, 9, 7, 5, 3, 1):
                step(dve.tensor_tensor(sp[:, 5, :], sp[:, 5, :], sp[:, 4, :], ALU.mult))
                step(dve.tensor_scalar(sp[:, 5, :], sp[:, 5, :], 2.0 / n, None, ALU.add))
            step(dve.tensor_tensor(sp[:, 5, :], sp[:, 5, :], sp[:, 3, :], ALU.mult))
            step(dve.tensor_tensor(sp[:, 2, :], sp[:, 2, :], sp[:, 5, :], ALU.add))
            dve.tensor_scalar(sp[:, 4, :], sp[:, 2, :], RG_C, None, ALU.mult).then_inc(sp_ready, 1)
            dve.tensor_scalar(sp[:, 5, :], sp[:, 2, :], -RG_C, None, ALU.mult).then_inc(sp_ready, 1)
            step(dve.memset(rxp[:, :, 0:3], 0.0))
            step(dve.memset(prod[:, :, 0:2], 0.0))
            dve.sem_inc(chunk_done, 2)

            scale(0, "g_mix", hn)

            def z_is(i, k):
                dve.wait_ge(z_evac, i * 14 + (Z_BANKS + k + 1))

            def conv4(i, a):
                z_is(i, a)
                c = i * 2 + a
                step(dve.tensor_scalar(xc[:, a, :], rxp[:, a, 0:T], pd("conv4_w", c), pd("conv4_b", c), ALU.mult, ALU.add))
                for k in range(1, 3):
                    fma(xc[:, a, :], rxp[:, a, k:k + T], pd("conv4_w", c + k * DC), xc[:, a, :])
                dve.scalar_tensor_tensor(out=xc[:, a, :], in0=rxp[:, a, 3:3 + T], scalar=pd("conv4_w", c + 3 * DC),
                                         in1=xc[:, a, :], op0=ALU.mult, op1=ALU.add).then_inc(xc_ready, 1)

            def conv3(i, a):
                z_is(i, 5 if a == 0 else 11)
                c = i * 2 + a
                step(dve.tensor_tensor(prod[:, a, 2:], zb["cc"][:, a, :], zb["cx"][:, a, :], ALU.mult))
                step(dve.tensor_scalar(zb["cc"][:, a, :], prod[:, a, 0:T], pd("conv3_w", c), None, ALU.mult))
                fma(zb["cc"][:, a, :], prod[:, a, 1:1 + T], pd("conv3_w", c + DC), zb["cc"][:, a, :])
                fma(zb["cc"][:, a, :], prod[:, a, 2:2 + T], pd("conv3_w", c + 2 * DC), zb["cc"][:, a, :])
                step(dve.tensor_tensor(zb["cb"][:, a, :], zb["cb"][:, a, :], zb["cc"][:, a, :], ALU.mult))

            def join(i, a):
                z_is(i, 7 if a == 0 else 13)
                step(dve.tensor_tensor(hs[:, a, :], hs[:, a, :], zb["ry"][:, a, :], ALU.mult))
                step(dve.tensor_tensor(hs[:, a, :], hs[:, a, :], zb["gr"][:, a, :], ALU.mult))
                step(dve.tensor_tensor(zb["cb"][:, a, :], zb["cb"][:, a, :], zb["gc"][:, a, :], ALU.mult))
                dve.tensor_tensor(merged[:, bass.ds(i * 2 + a, 1), :].rearrange("p a t -> p (a t)"), hs[:, a, :],
                                  zb["cb"][:, a, :], ALU.add).then_inc(chunk_done, 1)

            with dve.Fori(0, HEADS_RG) as i:
                step.enter(i, 32)
                conv4(i, 0)
                conv4(i, 1)
                conv3(i, 0)
                for a in range(2):
                    dve.wait_ge(th_ready, i * 2 + (a + 1))
                    step(dve.tensor_scalar(mlt[:, a, :], th[:, a, :], 1.0, None, ALU.add))
                    step(dve.reciprocal(mlt[:, a, :], mlt[:, a, :]))
                    dve.tensor_tensor(mlt[:, a, :], mlt[:, a, :], th[:, a, :], ALU.mult).then_inc(m2_ready, 1)
                dve.wait_ge(rg_evac, i * 4 + 5)
                dve.wait_ge(xc_ready, i * 2 + 2)
                for a in range(2):
                    step(dve.tensor_tensor(i_g[:, a, :], i_g[:, a, :], xc[:, a, :], ALU.mult))
                for a in range(2):
                    dve.wait_ge(mlt_ready, i * 2 + (a + 1))
                    dve.wait_ge(a_ready, i * 2 + (a + 1))
                    step(dve.tensor_tensor(i_g[:, a, :], i_g[:, a, :], mlt[:, a, :], ALU.mult))
                    step(dve.tensor_tensor_scan(out=hs[:, a, :], data0=a_t[:, a, :], data1=i_g[:, a, :], initial=0.0,
                                                op0=ALU.mult, op1=ALU.add))
                join(i, 0)
                conv3(i, 1)
                join(i, 1)
                step.leave(HEADS_RG)

            def residual(u, passes, units):
                with dve.Fori(0, passes) as i:
                    for j in range(4 // units):
                        dve.wait_ge(unit_done, i * 4 + (u + (j + 1) * units))
                        xs = x[:, bass.ds(i * (4 // units) + j, 1), :].rearrange("p a t -> p (a t)")
                        dve.tensor_tensor(xs, xs, ps[:, 3 + j, :], ALU.add).then_inc(x_add, 1)

            dve.sem_inc(x_add, 4)
            residual(U_OUT, 2, 1)
            dve.sem_inc(ff_act, 2)
            scale(1, "g_ffn", hn)
            step(dve.tensor_copy(ang[:, 2, :], posi[:, :]))
            for t, inv in enumerate(("inv_a", "inv_b")):
                a, k = ang[:, 0, :], ang[:, 1, :]
                step(dve.tensor_scalar(a, ang[:, 2, :], cc(inv), None, ALU.mult))
                step(dve.tensor_scalar(k, a, 1 / TWO_PI, ROUND, ALU.mult, ALU.add))
                step(dve.tensor_scalar(k, k, -ROUND, None, ALU.add))
                for part in TWO_PI_PARTS:
                    step(dve.scalar_tensor_tensor(out=a, in0=k, scalar=-part, in1=a, op0=ALU.mult, op1=ALU.add))
                step(dve.tensor_scalar(k, a, TWO_PI / 4, -TWO_PI, ALU.is_gt, ALU.mult))
                step(dve.scalar_tensor_tensor(out=k, in0=a, scalar=TWO_PI / 4, in1=k, op0=ALU.add, op1=ALU.add))
                dve.tensor_scalar(rope[:, 2 * t, :], k, PI_BELOW, -PI_BELOW, ALU.min, ALU.max).then_inc(rope_ang, 1)
                dve.tensor_scalar(rope[:, 2 * t + 1, :], a, PI_BELOW, -PI_BELOW, ALU.min, ALU.max).then_inc(rope_ang, 1)
                dve.wait_ge(rope_ang, 2 * t + 2)
            with dve.Fori(0, FC // 2) as i:
                for j in range(2):
                    dve.wait_ge(unit_done, i * 4 + (U_FF + 2 * j + 2))
                    dve.wait_ge(silu_done, i * 2 + (2 + j + 1))
                    dve.tensor_tensor(act[:, bass.ds(i * 2 + j, 1), :].rearrange("p a t -> p (a t)"), sg[:, j, :],
                                      ps[:, 2 * j + 1, :], ALU.mult).then_inc(ff_act, 1)
            dve.sem_inc(x_add, 2)
            residual(U_DOWN, 4, 2)
            scale(2, "g_ple", hn)
            dve.wait_ge(ple_evac, DC)
            for c in range(DC):
                dve.wait_ge(gate_done, c + 1)
                step(dve.tensor_tensor(gate[:, c % 2, :], gate[:, c % 2, :], pw[:, c, :], ALU.mult))
                dve.tensor_tensor(x[:, c, :], x[:, c, :], gate[:, c % 2, :], ALU.add).then_inc(x_add, 1)
            dve.wait_ge(x_add, X_BASE[U_GATE] + DC)
            scale(3, "g_final", x)
            scale(4, "norm1", hn)
            step(dve.tensor_scalar(pc("qk_gain", A_R), pc("qk_gain", A_R), A_D ** -0.5, None, ALU.mult))
            step(dve.tensor_scalar(pc("mla_gain", B_H), pc("mla_gain", B_H), B_QK ** -0.5, None, ALU.mult))
            step(dve.tensor_copy(identb[:, :], cc("ident")))
            step(dve.tensor_copy(causalb[:, :], cc("causal")))
            step(dve.tensor_copy(cmpb[:, :, :].rearrange("p a n -> p (a n)"), cc("cmp_mask")))
            for kv in range(2):
                dve.wait_ge(in_evac, 6 + 2 * kv)
                for j in range(CMP_LEN // 2):
                    o = dve.tensor_scalar(blk[:, kv, j, :].rearrange("p (g n) -> p g n", g=A_G),
                                          kcd[:, 2 * kv:2 * kv + 2, 2 * j:2 * j + (N_CMP - 1) * CMP_STRIDE + 1:CMP_STRIDE],
                                          pc("pos_w", at=j), None, ALU.add)
                o.then_inc(blk_ready, 1)
            scale(5, "lora_q", cq, src=cq)
            scale(6, "lora_kv", cq, src=cq, at=2)
            dve.wait_ge(in_evac, 14)
            dve.tensor_copy(mqk[B_NOPE:B_QK, B_H:, :],
                            kr[B_NOPE:B_QK, :].unsqueeze(1).to_broadcast([B_ROPE, B_H, T])).then_inc(rope_ready, 1)
            dve.wait_ge(rope_ready, 5)

            def rope_items(i, base, per, rows, src, gain, table, cols=T, sub=None):
                n = [(i * 2 if i is not None else 0) + (base + j + 1) for j in range(per)]
                at = [bass.ds(i * 2 + j, 1) if i is not None else slice(0, 1) for j in range(per)]
                v = [src[0:rows, at[j], 0:cols].rearrange("p a t -> p (a t)") for j in range(per)]
                cos, sin = (rope[0:rows, table + k, :] for k in range(2))

                def by(dst, a, tab):
                    if sub is None:
                        return dve.tensor_tensor(dst, a, tab, ALU.mult)
                    tab = tab[:, CMP_LEN - 1::CMP_STRIDE].unsqueeze(1).to_broadcast([rows, A_G, N_CMP])
                    two_d = lambda z: z.rearrange("p (g n) -> p g n", g=A_G)
                    return dve.tensor_tensor(two_d(dst), two_d(a), tab, ALU.mult)

                for j in range(per):
                    g = par[0:rows, bass.ds(i * 2 + (PAR[gain] + j), 1)] if i is not None \
                        else par[0:rows, PAR[gain]:PAR[gain] + 1]
                    dve.wait_ge(rrms, n[j])
                    step(dve.reciprocal(rst[0:rows, j, 0:cols], rst[0:rows, j, 0:cols]))
                    dve.scalar_tensor_tensor(out=xn[0:rows, j, 0:cols], in0=v[j], scalar=g, in1=rst[0:rows, j, 0:cols],
                                             op0=ALU.mult, op1=ALU.mult).then_inc(rxn, 1)
                for j in range(per):
                    dve.wait_ge(rrot, n[j])
                    step(by(rt[0:rows, j, 0:cols], ps[0:rows, 2 + j, 0:cols], sin))
                    dve.wait_ge(rxn, n[j])
                    step(by(xn[0:rows, j, 0:cols], xn[0:rows, j, 0:cols], cos))
                    dve.tensor_tensor(v[j], xn[0:rows, j, 0:cols], rt[0:rows, j, 0:cols], ALU.add).then_inc(rdone, 1)

            dve.sem_inc(rdone, 2)
            with dve.Fori(0, 3) as i:
                step.enter(i, 6)
                rope_items(i, 0, 2, P, qk, "qk_gain", 0)
                step.leave(3)
            rope_items(None, 6, 1, P, kcn, "kc_gain", 0, A_G * N_CMP, True)
            with dve.Fori(0, B_H) as i:
                step.enter(i, 6)
                rope_items(i, 7, 2, B_QK, mqk, "mla_gain", 2)
                step.leave(B_H)

            def attend(i, units, base):
                per = len(units)
                for s in range(per + 1):
                    if s < per:
                        g, kind, qt = units[s]
                        nk = N_CMP if kind == "cmp" else (qt + 1) * P
                        dve.wait_ge(at_s, i * per + (base + s + 1))
                        dve.tensor_reduce(st[:, s % 3, 0:1], ps[:, s % 3, 0:nk], AX_X, ALU.max, negate=True)\
                            .then_inc(at_max, 1)
                    if s >= 1:
                        u = s - 1
                        g, kind, qt = units[u]
                        nk = N_CMP if kind == "cmp" else (qt + 1) * P
                        p_ = pr[:, u % 3, 0:nk]
                        dve.wait_ge(at_exp, i * per + (base + u + 1))
                        step(dve.reciprocal(st[:, u % 3, 2:3], st[:, u % 3, 1:2]))
                        if kind == "cmp" and qt == 0:
                            step(dve.tensor_tensor(p_, p_, cc("cmp_seen"), ALU.mult))
                        if kind == "mla":
                            o = dve.tensor_scalar(p_, p_, st[:, u % 3, 2:3], None, ALU.mult)
                        else:
                            col = 2 * P + g * A_R * 3 + ("cmp", "slc", "win").index(kind)
                            o = dve.tensor_scalar(p_, p_, st[:, u % 3, 2:3],
                                                  vtok[:, qt, bass.ds(i * 3 + col, 1)], ALU.mult, ALU.mult)
                        o.then_inc(at_scale, 1)

            dve.wait_ge(tok_evac, 2 * TT)
            with dve.Fori(0, A_R) as i:
                step.enter(i, len(NSA) + 2)
                attend(i, NSA, S_NSA)
                step.leave(A_R)
            with dve.Fori(0, B_H // 2) as i:
                step.enter(i, len(MLA))
                attend(i, MLA, S_MLA)
                step.leave(B_H // 2)
            scale(7, "out_gain", oall, src=oall)
            scale(8, "out_gain", oall, src=oall, at=4, g_at=4)
            dve.sem_inc(x_add, 4)
            residual(U_OUT2, 2, 1)
            scale(9, "norm2", hn)
            dve.wait_ge(qs_used, 2 * E_H)
            step(dve.tensor_copy(ssq[:, :, :].rearrange("p a n -> p (a n)"), ps[:, 6, 0:2 * TT * E_H]))
            dve.tensor_tensor(ssq[:, 0, :], ssq[:, 0, :], ssq[:, 1, :], ALU.add).then_inc(ssq_sum, 1)
            dve.wait_ge(ssq_sqrt, 1)
            dve.reciprocal(ssq[:, 0, :], ssq[:, 0, :]).then_inc(rs_ready, 1)

            def top16(vals, idx, src, tmp):
                step(dve.max(vals[:, 0:8], src))
                step(dve.max_index(idx[:, 0:8], vals[:, 0:8], src))
                step(dve.match_replace(tmp, vals[:, 0:8], src, NEG_HUGE))
                step(dve.max(vals[:, 8:16], tmp))
                step(dve.max_index(idx[:, 8:16], vals[:, 8:16], tmp))

            bc = [P, E_H, E_K, E_K]
            flat = lambda z: z.rearrange("p a b c -> p (a b c)")
            for i in range(TT):
                dve.wait_ge(sk_evac, i * 8 + 8)
                for h in range(E_H):
                    for k in range(2):
                        src = s_sb[:, slice(i, i + 1), 2 * h + k, :].rearrange("p a n -> p (a n)")
                        top16(tv[:, k, h, :], ti[:, k, h, :], src, tk[:, 0:N_KEYS])
                    step(dve.tensor_tensor(cand[:, :, :], tv[:, 0, h, :].unsqueeze(2).to_broadcast([P, E_K, E_K]),
                                           tv[:, 1, h, :].unsqueeze(1).to_broadcast([P, E_K, E_K]), ALU.add))
                    top16(cv[:, h, :], ci[:, h, :], cand[:, :, :].rearrange("p a b -> p (a b)"), tk[:, :])
                dve.tensor_tensor(ce[:, :, :], cv[:, :, :], cv[:, :, 0:1].to_broadcast([P, E_H, E_K]), ALU.subtract)\
                    .then_inc(tk_sub, 1)
                step(dve.tensor_copy(flat(tif[:, :, :, :]), flat(ti[:, :, :, :])))
                step(dve.tensor_scalar(cm[:, 0, :, :], ci[:, :, :], 4, None, ALU.logical_shift_right))
                step(dve.tensor_scalar(cm[:, 1, :, :], ci[:, :, :], 15, None, ALU.bitwise_and))
                step(dve.tensor_copy(flat(cmf[:, :, :, :]), flat(cm[:, :, :, :])))
                for k in range(2):
                    step(dve.tensor_tensor(oh[:, :, :, :], cmf[:, k, :, :].unsqueeze(3).to_broadcast(bc),
                                           cc("iota16").unsqueeze(1).unsqueeze(1).to_broadcast(bc), ALU.is_equal))
                    step(dve.tensor_tensor(oh[:, :, :, :], oh[:, :, :, :],
                                           tif[:, k, :, :].unsqueeze(2).to_broadcast(bc), ALU.mult))
                    step(dve.tensor_reduce(sel[:, i:i + 1, k, :].rearrange("p a (h k) -> p (a h) k", h=E_H),
                                           oh[:, :, :, :], AX_X, ALU.add))
                dve.wait_ge(tk_exp, i + 1)
                step(dve.tensor_reduce(gs[:, 0, :], ce[:, :, :], AX_X, ALU.add))
                step(dve.reciprocal(gs[:, 1, :], gs[:, 0, :]))
                dve.tensor_tensor(sel[:, i:i + 1, 2, :].rearrange("p a (h k) -> p (a h) k", h=E_H), ce[:, :, :],
                                  gs[:, 1, :].unsqueeze(2).to_broadcast([P, E_H, E_K]), ALU.mult).then_inc(sel_ready, 1)
                dve.wait_ge(sel_ready, i + 1)
            dve.wait_ge(selt_done, 1)
            step(dve.tensor_copy(n1t[:, :], ps[:, 4, :]))
            step(dve.tensor_copy(n2q[:, :], ps[:, 5, :]))
            step(dve.tensor_copy(g3[:, 0, :], ps[:, 6, :]))
            step(dve.tensor_tensor(gf[:, 0, :], ps[:, 6, :], g3[:, 0, :], ALU.subtract))
            step(dve.tensor_copy(g3[:, 1, :], gf[:, 0, :]))
            step(dve.tensor_tensor(gf[:, 1, :], gf[:, 0, :], g3[:, 1, :], ALU.subtract))
            step(dve.tensor_copy(g3[:, 2, :], gf[:, 1, :]))
            dve.sem_inc(gx_done, 2)
            dve.sem_inc(gx_evac, 2)
            dve.sem_inc(y_add, HB)
            dve.wait_ge(iota_ready, 1)
            with dve.Fori(0, NQ) as q:
                with dve.Fori(0, T // GB // 2) as b:
                    for j in range(2):
                        tok = bass.ds(b * (2 * GB) + j * GB, GB)
                        dve.wait_ge(gx_done, q * (T // GB) + (b * 2 + (j + 1)))
                        dve.tensor_tensor(oh1[:, j, :, :], n1t[:, tok].unsqueeze(1).to_broadcast([P, N_KEYS, GB]),
                                          iota[:, :, :], ALU.is_equal)
                        dve.tensor_tensor(oh2[:, j, 0, :, :], n2q[:, tok].unsqueeze(1).to_broadcast([P, QN, GB]),
                                          iota[:, 0:QN, :], ALU.is_equal).then_inc(oh_eq, 1)
                        dve.wait_ge(oh_eq, q * (T // GB) + (b * 2 + (j + 1)))
                        for k in range(3):
                            o = dve.tensor_tensor(oh2[:, j, 1 + k, :, :], oh2[:, j, 0, :, :],
                                                  g3[:, k, tok].unsqueeze(1).to_broadcast([P, QN, GB]), ALU.mult)
                        o.then_inc(oh_ready, 1)
                    for j in range(2):
                        g = gb[:, :, bass.ds(b * (2 * GB) + j * GB, GB)]
                        dve.wait_ge(gelu_done, q * E_A + (4 + E_A))
                        dve.wait_ge(gx_done, q * (T // GB) + (b * 2 + (2 + j + 1)))
                        dve.tensor_tensor(g, g, ps[:, 4 + j, :].rearrange("p (t n) -> p n t", n=QN), ALU.mult)\
                            .then_inc(gx_evac, 1)
                dve.wait_ge(oh_ready, q * (T // GB) + T // GB)
                dve.tensor_scalar(n2q[:, :], n2q[:, :], -float(QN), None, ALU.add).then_inc(n2_next, 1)
                for half in range(2):
                    with dve.Fori(0, E_Y // 4) as i:
                        dve.wait_ge(n2_next, q + 1)
                        for j in range(4):
                            dve.wait_ge(wh_ready, q * (2 * E_Y) + i * 4 + (half * E_Y + j + 1))
                            dve.tensor_tensor(wsp[:, j % 2, 1, :],
                                              gb[:, bass.ds(i * 8 + 2 * j, 2), :].rearrange("p a t -> p (a t)"),
                                              wsp[:, j % 2, 0, :].bitcast(F32), ALU.subtract).then_inc(wl_ready, 1)
                    for c in range(HB):
                        dve.wait_ge(e_done, q * E_Q + (2 + E_A + (half + 1) * E_Y))
                        xs = x[:, half * HB + c, :]
                        dve.tensor_tensor(xs, xs, ps[:, 4 + c, :], ALU.add).then_inc(y_add, 1)

        @block.gpsimd
        def _(pool):
            pool.iota(iota[:, :, :], pattern=[[1, N_KEYS], [0, GB]], base=0, channel_multiplier=0,
                      allow_small_or_imprecise_dtypes=True).then_inc(iota_ready, 1)
            pool.wait_ge(rdone, 2 + 7)
            with pool.Fori(0, A_R) as i:
                pool.wait_ge(at_out, i + 1)
                pool.tensor_copy(q_cur[:, 0, :], qk[:, bass.ds(i, 1), :].rearrange("p a t -> p (a t)")).then_inc(cur_ready, 1)
            pool.wait_ge(rdone, 2 + 7 + 2 * B_H)
            pool.wait_ge(mv_evac, TT)
            with pool.Fori(0, B_H // 2) as i:
                pool.wait_ge(at_out, i + (A_R + 1))
                for h in range(2):
                    for dst, at in ((q_cur, h), (k_cur, B_H + h)):
                        pool.tensor_copy(dst[0:B_QK, h, :], mqk[:, bass.ds(i * 2 + at, 1), :].rearrange("p a t -> p (a t)"))\
                            .then_inc(cur_ready, 1)
                    pool.tensor_copy(v_cur[:, h, :, :], vm[:, :, bass.ds(i * (2 * B_V) + h * B_V, B_V)]).then_inc(cur_ready, 1)
            for c in range(DC):
                pool.wait_ge(hh_ready, c + 1)
                pool.tensor_tensor(hl[:, c, :], hn[:, c, :], hh[:, c, :].bitcast(F32), ALU.subtract).then_inc(hl_ready, 1)
            with pool.Fori(0, NQ * E_Q // RING) as i:
                for j in range(RING):
                    pool.wait_ge(hi_done, i * RING + (j + 1))
                    pool.tensor_tensor(spl[:, j % 2, 1, :], ring[:, j, 0:D], spl[:, j % 2, 0, :].bitcast(F32),
                                       ALU.subtract).then_inc(lo_done, 1)


S_NSA = 0
S_MLA = A_R * A_G * 3 * TT
TWO_PI = 6.283185307179586
TWO_PI_PARTS = (6.28125, 0.00193500518798828125, 3.0199159819e-7)
ROUND = 12582912.0
PI_BELOW = 3.1415925
X_BASE = {U_OUT: 0, U_DOWN: 4 + DC, U_GATE: 4 + DC + 2 + DC, U_OUT2: 4 + DC + 2 + DC + DC}


def _feature_major(a):
    return np.ascontiguousarray(a.T.reshape(-1, P, a.shape[0]).transpose(1, 0, 2))


def _unit(w):
    u = w.reshape(-1, P, w.shape[1]).transpose(1, 0, 2).reshape(P, -1)
    return np.pad(u, ((0, 0), (0, UNIT - u.shape[1])))


def _chan(v):
    return v.reshape(-1, P).T


def _cat(ws):
    u = np.concatenate([w.reshape(-1, P, w.shape[1]).transpose(1, 0, 2).reshape(P, -1) for w in ws], 1)
    return np.pad(u, ((0, 0), (0, UNIT - u.shape[1])))


def _by_r(w):
    return w.reshape(A_G, A_R, A_D, -1).transpose(1, 0, 2, 3).reshape(A_H * A_D, -1)


def _rotation(width, blocks, half):
    m = np.zeros((P, width), np.float32)
    for b in blocks:
        for i in range(half):
            m[b + half + i, b + i] = -1.0
            m[b + i, b + half + i] = 1.0
    return m


def _constants():
    c = np.zeros((P, N_CST), np.float32)
    put = lambda name, v: c.__setitem__((slice(None), slice(*CST[name])), v)
    row = np.arange(P)
    put("ones", 1.0)
    put("ident", np.eye(P))
    put("blk", (row[:, None] // A_D == row[None] // A_D))
    put("rot_a", _rotation(P, (0, A_D), A_ROT // 2))
    put("rot_b", _rotation(B_QK, (B_NOPE,), B_ROPE // 2))
    put("causal", np.where(row[None] <= row[:, None], 0.0, MASKED))
    tok = np.arange(TT)[None, :, None] * P + row[:, None, None]
    end = np.arange(N_CMP)[None, None] * CMP_STRIDE + CMP_LEN - 1
    put("cmp_mask", np.where(end <= tok, 0.0, MASKED).reshape(P, -1))
    put("cmp_seen", (end <= tok)[:, 0])
    inv = lambda n: np.float32(ROPE_THETA) ** (-np.arange(0, n, 2, dtype=np.float32) / n)
    a = np.zeros(P, np.float32)
    b = np.zeros(P, np.float32)
    for base in (0, A_D):
        a[base:base + A_ROT] = np.tile(inv(A_ROT), 2)
    b[B_NOPE:B_QK] = np.tile(inv(B_ROPE), 2)
    put("inv_a", a[:, None])
    put("inv_b", b[:, None])
    put("iota16", np.arange(E_K)[None])
    return c


def _stream(n):
    units = []
    w_in = n["w_in"][0]
    for h in range(HEADS_RG):
        us = {}
        for k, (name, a) in enumerate(Z_ORDER):
            c = Z_SPLIT[name] * D + (2 * h + a) * P
            us[Z_UNIT[k]] = _unit(w_in[:, c:c + P])
        for g, name in enumerate(("w_rg_r", "w_rg_i")):
            us[RG_UNIT + g] = _unit(n[name][0, h])
        units += [us[k] for k in range(16)]
    cols = lambda w: [_unit(w[:, c * P:(c + 1) * P]) for c in range(w.shape[1] // P)]
    units += cols(n["w_out"][0])
    gu = cols(n["w_gate_up"][0])
    for c in range(FC):
        units += [gu[c], gu[FC + c]]
    wd = n["w_down"][0]
    for c in range(DC):
        for h in range(2):
            units.append(_unit(wd[h * FF // 2:(h + 1) * FF // 2, c * P:(c + 1) * P]))
    wp = n["w_ple"][0]
    for g in range(2):
        w = wp[:, g * 4 * P:(g + 1) * 4 * P].reshape(2, P, 4, P).transpose(1, 2, 0, 3).reshape(P, -1)
        units.append(np.pad(w, ((0, 0), (0, UNIT - w.shape[1]))))
    units += cols(n["w_ple_gate"][0])
    w2 = n["w_in_2"][0]
    at = np.cumsum((0, 512, 128, 128, 128, 128, 128, 128, 24, Q_LORA, 128, B_ROPE))
    q, kc, vc, ks, vs, kw, vw, gt, cq, ckv, krw = (w2[:, at[k]:at[k + 1]] for k in range(11))
    for r in range(A_R):
        units.append(_unit(np.concatenate([q[:, (g * A_R + r) * A_D:(g * A_R + r + 1) * A_D] for g in range(A_G)], 1)))
    for w in (kc, vc):
        for g in range(A_G):
            units.append(_unit(np.concatenate([w[:, g * A_D:(g + 1) * A_D]] * 2, 1)))
    units += [_unit(ks), _unit(kw), _unit(cq[:, :P]), _unit(cq[:, P:]), _unit(ckv),
              _unit(np.pad(krw, ((0, 0), (B_NOPE, P - B_QK))))]
    tok = np.concatenate([vs, vw, gt], 1)
    units += [_unit(tok[:D // 2]), _unit(tok[D // 2:])]
    for w in (n["cmp_k_w1_2"][0], n["cmp_v_w1_2"][0]):
        for m in range(2):
            for h in range(2):
                units.append(_unit(w[h * 1024:(h + 1) * 1024, m * P:(m + 1) * P]))
    k2, v2 = n["cmp_k_w2_2"][0], n["cmp_v_w2_2"][0]
    units.append(_cat([np.concatenate([k2, k2], 1), v2]))
    uq = n["mla_w_uq_2"][0]
    units += [_unit(uq[:, :4 * B_QK]), _unit(uq[:, 4 * B_QK:])]
    ukv = n["mla_w_ukv_2"][0].reshape(P, B_H, B_NOPE + B_V)
    units.append(_unit(np.concatenate([ukv[:, :, :B_NOPE].reshape(P, -1), ukv[:, :, B_NOPE:].reshape(P, -1)], 1)))
    wo = n["w_out_2"][0]
    units += cols(np.concatenate([_by_r(wo[:A_H * A_D]), wo[A_H * A_D:]]))
    units += cols(n["peer_w_q_2"][0])
    keys = n["peer_sub_keys_2"][0].reshape(2 * E_H, N_KEYS, N_KEYS).transpose(2, 0, 1)
    units += [_unit(keys[:, :E_H].reshape(P, -1)), _unit(keys[:, E_H:].reshape(P, -1))]
    assert len(units) == N_UNITS
    return np.stack(units)


def _twice(v):
    return np.concatenate([v, v])[:, None]


def _rows(v):
    return np.pad(v, (0, P - v.size))[:, None]


def kernel(**inputs):
    import concourse.bacc as bacc
    from concourse.bass_utils import run_bass_kernel_spmd

    n = {k: np.asarray(v) for k, v in inputs.items()}
    par = np.concatenate(
        [_chan(n["g_mix"][0]), _chan(n["lru_lambda"][0])] + [_chan(n["conv4_w"][0, k]) for k in range(4)]
        + [_chan(n["conv4_b"][0]), _chan(n["b_rg_r"][0].reshape(-1)), _chan(n["b_rg_i"][0].reshape(-1))]
        + [_chan(n["conv3_w"][0, k]) for k in range(3)]
        + [_chan(n["g_ffn"][0]), _chan(n["g_ple"][0]), _chan(n["g_final"]), np.full((P, 1), EPS, np.float32)]
        + [_chan(n["norm1_gain_2"][0])] + [_twice(n["nsa_q_gain_2"][0])] * A_R + [_twice(n["nsa_ks_gain_2"][0])]
        + [_twice(n["nsa_kw_gain_2"][0]), _twice(n["nsa_kc_gain_2"][0]), _chan(n["cmp_pos_2"][0].reshape(-1))]
        + [_chan(n["mla_q_lora_gain_2"][0]), _chan(n["mla_kv_lora_gain_2"][0])]
        + [_rows(n["mla_q_gain_2"][0])] * B_H + [_rows(n["mla_k_gain_2"][0])] * B_H
        + [_chan(_by_r(n["out_gain_a_2"][0][:, None])[:, 0]), _chan(n["out_gain_b_2"][0]), _chan(n["norm2_gain_2"][0])],
        axis=1)
    arrays = {
        "x_in": _feature_major(n["x"][0]), "par_in": np.ascontiguousarray(par),
        "p_in": _feature_major(n["p"][0, 0]), "cst_in": _constants(), "stream_in": _stream(n),
        "pos_in": np.ascontiguousarray(np.broadcast_to(n["positions_2"].astype(np.int32), (P, T))),
        "u_in": np.ascontiguousarray(n["peer_u_2"][0].reshape(N_KEYS, N_KEYS, DC, P).transpose(1, 3, 2, 0)
                                     .reshape(N_KEYS, P, D)),
        "v_in": np.ascontiguousarray(n["peer_v_2"][0].reshape(N_KEYS, NQ, E_Y, 2, 2, HB * P).transpose(1, 4, 2, 0, 3, 5)
                                     .reshape(NQ * 2 * E_Y, P, D)),
    }
    nc = bacc.Bacc("TRN2", target_bir_lowering=False, num_devices=1)
    aps = [nc.dram_tensor(k, a.shape, mybir.dt.from_np(a.dtype), kind="ExternalInput").ap() for k, a in arrays.items()]
    out = nc.dram_tensor("out", (P, DC, T), F32, kind="ExternalOutput").ap()
    build(nc, *aps, out)
    r = run_bass_kernel_spmd(nc, [arrays], core_ids=[0])
    return np.ascontiguousarray(r.results[0]["out"].transpose(1, 0, 2).reshape(D, T).T)[None]
```

```python
from contextlib import ExitStack

import numpy as np

import concourse.bass as bass
from concourse import mybir

ALU = mybir.AluOpType
ACT = mybir.ActivationFunctionType
F32 = mybir.dt.float32
BF16 = mybir.dt.bfloat16
F32R = mybir.dt.float32r
AX_X = mybir.AxisListType.X

P = 128
T = 512
D = 1024
DC = D // P
EPS = 1e-6
HEADS_RG = 4
RG_C = 8.0
FF = 2816
FC = FF // P
A_H, A_G, A_D = 8, 2, 64
A_R = A_H // A_G
A_ROT = 16
CMP_LEN, CMP_STRIDE = 32, 16
N_CMP = (T - CMP_LEN) // CMP_STRIDE + 1
B_H, B_NOPE, B_ROPE, B_V = 8, 64, 32, 64
B_QK = B_NOPE + B_ROPE
Q_LORA = 256
TT = T // P
VW = 2 * A_G * A_D + 3 * A_H
ROPE_THETA = 500000.0
MASKED = -1e30
E_H, E_K, N_KEYS = 8, 16, 128
NEG_HUGE = -3.0e38
assert T // 64 <= 16 and T <= 512
QN = 32
GB = 16
NQ = N_KEYS // QN
HB = 4
E_A = QN
E_Y = QN // 2
E_Q = E_A + 2 * E_Y
EARLY = 24
BLOCKS = T // GB
STORE = 4
B_GROUPS = BLOCKS // (2 * STORE)
G_SLOTS = 4
X_LOADS = 4
RING = 4
UNIT = FC // 2 * P

PAR = {}


def _columns():
    at = 0
    for name, n in (("g_mix", DC), ("lam", DC), ("conv4_w", 4 * DC), ("conv4_b", DC), ("b_r", DC), ("b_i", DC),
                    ("conv3_w", 3 * DC), ("g_ffn", DC), ("g_ple", DC), ("g_final", DC), ("eps", 1),
                    ("norm1", DC), ("qk_gain", A_R + 2), ("kc_gain", 1), ("pos_w", CMP_LEN // 2), ("lora_q", 2),
                    ("lora_kv", 1), ("mla_gain", 2 * B_H), ("out_gain", DC), ("norm2", DC)):
        PAR[name] = at
        at += n
    return at


N_PAR = _columns()

U_BLOCK = 0
U_OUT = U_BLOCK + HEADS_RG * 16
U_FF = U_OUT + DC
U_DOWN = U_FF + 2 * FC
U_PLE = U_DOWN + 2 * DC
U_GATE = U_PLE + 2
U_END1 = U_GATE + DC
U_IN2 = U_END1
U_TOK = U_IN2 + 14
U_CMP = U_TOK + 2
U_CMP2 = U_CMP + 8
U_UQ = U_CMP2 + 1
U_UKV = U_UQ + 2
U_OUT2 = U_UKV + 1
U_WQ = U_OUT2 + DC
U_KEYS = U_WQ + 2 * E_H
U_EXP = U_KEYS + 2
N_UNITS = U_EXP

CST = {}


def _cst():
    at = 0
    for name, n in (("ones", P), ("ident", P), ("blk", P), ("rot_a", P), ("rot_b", B_QK), ("causal", P),
                    ("cmp_mask", TT * N_CMP), ("cmp_seen", N_CMP), ("inv_a", 1), ("inv_b", 1), ("iota16", E_K)):
        CST[name] = (at, at + n)
        at += n
    return at


N_CST = _cst()
N_SPLIT = U_TOK + 2
SPLIT = 4 * VW
PARTED = [0, 1, 2, 4, 9]
NORMS = [DC, DC, DC, DC, DC, 2, 1, 4, 4, DC]
NB = [sum(NORMS[:n]) for n in range(len(NORMS) + 1)]

Z_ORDER = [("rx", 0), ("rx", 1), ("ry", 0), ("cb", 0), ("cc", 0), ("cx", 0),
           ("gr", 0), ("gc", 0), ("ry", 1), ("cb", 1), ("cc", 1), ("cx", 1), ("gr", 1), ("gc", 1)]
Z_UNIT = [0, 1, 2, 3, 4, 5, 8, 9, 10, 11, 12, 13, 14, 15]
Z_SPLIT = {"rx": 0, "ry": 1, "cb": 2, "cc": 3, "cx": 4, "gr": 5, "gc": 6}
RG_UNIT = 6
Z_BANKS = 7


class Order:

    def __init__(self, eng, sem):
        self.eng, self.sem, self.base, self.n, self.per = eng, sem, 0, 0, 0

    def __call__(self, ins):
        ins.then_inc(self.sem, 1)
        self.n += 1
        self.eng.wait_ge(self.sem, self.base + self.n)

    def enter(self, i, per):
        self.start, self.per = self.base + self.n, per
        self.base, self.n = i * per + self.start, 0

    def leave(self, passes):
        assert self.n == self.per, self.n
        self.base, self.n = self.start + passes * self.per, 0


def build(nc, xT_in, par_in, pT_in, cst_in, stream, pos_in, u_in, v_in, out, dense):
    with ExitStack() as ctx:
        def sb(name, shape, dt=F32, c=ctx):
            return c.enter_context(nc.sbuf_tensor(name, shape, dt))

        def sem(name):
            return ctx.enter_context(nc.semaphore(name))

        ps = ctx.enter_context(nc.psum_tensor("ps", [P, 8, T], F32))
        ring = sb("ring", [P, RING, UNIT])
        par = sb("par", [P, N_PAR])
        cst = sb("cst", [P, N_CST])
        ones = cst[:, 0:P]
        x = sb("x", [P, DC, T])
        rstd = sb("rstd", [P, T])
        zero = sb("zero", [P, 1])

        identb = sb("identb", [P, P], BF16)
        causalb = sb("causalb", [P, P], BF16)
        cmpb = sb("cmpb", [P, TT, N_CMP], BF16)

        iota = sb("iota", [P, N_KEYS, GB], BF16)
        hnt = sb("hnt", [P, 2, T])
        spl = sb("spl", [P, 2, 2, SPLIT], F32R)
        lat = ExitStack()
        mqk = sb("mqk", [B_QK, 2 * B_H, T], c=lat)
        lat.close()
        hh = sb("hh", [P, DC, T], F32R)
        hl = sb("hl", [P, DC, T], F32R)
        both = ExitStack()
        rope = sb("rope", [P, 4, T], c=both)

        one = ExitStack()
        merged = sb("merged", [P, DC, T], c=one)
        pw = merged
        pT = sb("pT", [P, 2, T], c=one)
        posi = sb("posi", [P, T], mybir.dt.int32, c=one)
        ang = sb("ang", [P, 3, T], c=one)
        sp = sb("sp", [P, 6, DC], c=one)
        rg = ExitStack()
        rxp = sb("rxp", [P, 2, 3 + T], c=rg)
        prod = sb("prod", [P, 2, 2 + T], c=rg)
        zb = {n: sb(f"z_{n}", [P, 2, T], c=rg) for n in ("ry", "cb", "cc", "cx", "gr", "gc")}
        xc = sb("xc", [P, 2, T], c=rg)
        r_g = sb("r_g", [P, 2, T], c=rg)
        i_g = sb("i_g", [P, 2, T], c=rg)
        a_t = sb("a_t", [P, 2, T], c=rg)
        th = sb("th", [P, 2, T], c=rg)
        mlt = sb("mlt", [P, 2, T], c=rg)
        hs = sb("hs", [P, 2, T], c=rg)
        rg.close()
        act = sb("act", [P, FC, T], c=one)
        sg = sb("sg", [P, 2, T], c=one)
        gate = sb("gate", [P, 2, T], c=one)
        sq1 = sb("sq1", [P, DC, T], c=one)
        one.close()

        two = ExitStack()
        qk = sb("qk", [P, A_R + 2, T], c=two)
        kcn = sb("kcn", [P, 1, A_G * N_CMP], c=two)
        vct = sb("vct", [N_CMP, A_G, A_D], c=two)
        vtok = sb("vtok", [P, TT, VW], c=two)
        sq2 = sb("sq2", [P, DC, T], c=two)
        vm = sb("vm", [P, TT, B_H * B_V], c=two)
        pre = ExitStack()
        kcd = sb("kcd", [P, 4, T], c=pre)
        blk = sb("blk", [P, 2, CMP_LEN // 2, A_G * N_CMP], c=pre)
        hid = sb("hid", [P, 2, 2, A_G * N_CMP], c=pre)
        cq = sb("cq", [P, 3, T], c=pre)
        kr = sb("kr", [P, T], c=pre)
        sqt = sb("sqt", [P, 2, T], c=pre)
        rst = sb("rst", [P, 2, T], c=pre)
        xn = sb("xn", [P, 2, T], c=pre)
        rt = sb("rt", [P, 2, T], c=pre)
        pre.close()
        q_cur = sb("q_cur", [P, 2, T], c=two)
        v_cur = sb("v_cur", [P, 2, TT, B_V], c=two)
        pr = sb("pr", [P, 3, T], c=two)
        pt = sb("pt", [P, 2, TT, T], c=two)
        st = sb("st", [P, 3, 4], c=two)
        oall = sb("oall", [P, DC, T], c=two)
        two.close()
        both.close()

        ex = ExitStack()
        ch = ExitStack()
        qp = sb("qp", [P, 2 * E_H, T], c=ch)
        sb("early", [P, EARLY - 16, T], c=ch)
        s_sb = sb("s_sb", [P, TT, 2 * E_H, N_KEYS], c=ch)
        ssq = sb("ssq", [P, 2, TT * E_H], c=ch)
        qs_mem = ExitStack()
        qs = sb("qs", [P, 4, T], c=qs_mem)
        qs_mem.close()
        cand = sb("cand", [P, E_H, E_K, E_K], c=ch)
        tv = sb("tv", [P, 2, E_H, E_K], c=ch)
        ti = sb("ti", [P, 2, E_H, E_K], mybir.dt.uint32, c=ch)
        tif = sb("tif", [P, 2, E_H, E_K], BF16, c=ch)
        cv = sb("cv", [P, E_H, E_K], c=ch)
        ci = sb("ci", [P, E_H, E_K], mybir.dt.uint32, c=ch)
        cm = sb("cm", [P, 2, E_H, E_K], mybir.dt.uint32, c=ch)
        cmf = sb("cmf", [P, 2, E_H, E_K], BF16, c=ch)
        ce = sb("ce", [P, E_H, E_K], c=ch)
        oh = sb("oh", [P, E_H, E_K, E_K], BF16, c=ch)
        places = sb("places", [P, E_K], BF16, c=ch)
        sel = sb("sel", [P, TT, 3, E_H * E_K], c=ch)
        gs = sb("gs", [P, 2, E_H], c=ch)
        ch.close()
        gb = sb("gb", [P, QN, T], c=ex)
        stage_mem = ExitStack()
        stage = sb("stage", [P, 2, QN, STORE * GB], c=stage_mem)
        stage_mem.close()
        wsp = sb("wsp", [P, 2, 2, 2 * T], F32R, c=ex)
        hot = ExitStack()
        oh1 = sb("oh1", [P, 2, N_KEYS, GB], BF16, c=hot)
        oh2 = sb("oh2", [P, 2, 4, QN, GB], BF16, c=hot)
        hot.close()
        gw = sb("gw", [P, G_SLOTS, 2, T], c=ex)
        n1t = sb("n1t", [P, T], BF16, c=ex)
        n2q = sb("n2q", [P, T], BF16, c=ex)
        g3 = sb("g3", [P, 3, T], BF16, c=ex)
        gf = sb("gf", [P, 2, T], c=ex)
        ex.close()

        in_evac, tok_evac, blk_ready, hid_ready = sem("in_evac"), sem("tok_evac"), sem("blk_ready"), sem("hid_ready")
        kc_evac, m_done, m_evac, mv_evac = sem("kc_evac"), sem("m_done"), sem("m_evac"), sem("mv_evac")
        rope_ang, rope_ready = sem("rope_ang"), sem("rope_ready")
        rsq, rss, rrms, rxn, rrot, rdone = (sem(f"rope_{v}") for v in ("sq", "ss", "rms", "xn", "rot", "done"))
        cur_ready = sem("cur_ready")
        at_s, at_max, at_exp, at_scale, at_t, at_ev, at_pv, at_out = (
            sem(f"at_{v}") for v in ("scores", "max", "exp", "scale", "transposed", "evacuated", "pv", "out"))
        qp_evac, ssq_sqrt, sk_done, sk_evac, rs_ready = (
            sem(v) for v in ("qp_evac", "ssq_sqrt", "sk_done", "sk_evac", "rs_ready"))
        tk_sub, tk_exp, sel_ready, selt_done = (sem(v) for v in ("tk_sub", "tk_exp", "sel_ready", "selt_done"))
        oh_eq, n2_next, zero_ready = sem("oh_eq"), sem("n2_next"), sem("zero_ready")
        iota_ready, oh_ready, gx_done, gx_evac = (sem(v) for v in ("iota_ready", "oh_ready", "gx_done", "gx_evac"))
        hi_done, lo_done, e_done, hh_ready, hl_ready = (
            sem(v) for v in ("hi_done", "lo_done", "e_done", "hh_ready", "hl_ready"))
        wt_high, wt_low = sem("wt_high"), sem("wt_low")
        wh_ready, wl_ready, qs_used, ssq_sum = (sem(v) for v in ("wh_ready", "wl_ready", "qs_used", "ssq_sum"))
        gelu_done, y_add, y_part, mul_done = (sem(v) for v in ("gelu_done", "y_add", "y_part", "mul_done"))
        g_stored = [sem(f"g_stored{k}") for k in range(2)]
        gw_ready = [sem(f"gw_ready{k}") for k in range(G_SLOTS)]
        w_ready = [sem(f"w_ready{s}") for s in range(RING)]
        unit_done = sem("unit_done")
        loaded, p_loaded = sem("loaded"), sem("p_loaded")
        x_loaded = [sem(f"x_loaded{k}") for k in range(X_LOADS)]
        dve_order = sem("dve_order")
        sq_ready, ss_ready, rms_ready, hn_ready = sem("sq_ready"), sem("ss_ready"), sem("rms_ready"), sem("hn_ready")
        z_evac, xc_ready, rg_ready, rg_evac = sem("z_evac"), sem("xc_ready"), sem("rg_ready"), sem("rg_evac")
        th_ready, m2_ready, mlt_ready, a_ready = sem("th_ready"), sem("m2_ready"), sem("mlt_ready"), sem("a_ready")
        chunk_done, sp_exp, sp_ready, sp_abs = sem("chunk_done"), sem("sp_exp"), sem("sp_ready"), sem("sp_abs")
        silu_done, ff_act = sem("silu_done"), sem("ff_act")
        x_add = sem("x_add")
        ple_evac, gate_done = sem("ple_evac"), sem("gate_done")
        out_done = sem("out_done")

        def pc(name, n=1, at=0):
            return par[:, PAR[name] + at:PAR[name] + at + n]

        def cc(name, rows=P):
            a, b = CST[name]
            return cst[0:rows, a:b]

        NSA = [(g, b, qt) for g in range(A_G) for b in ("cmp", "slc", "win") for qt in range(TT)]
        MLA = [(h, "mla", qt) for h in range(2) for qt in range(TT)]

        def pd(name, idx):
            return par[:, bass.ds(idx + PAR[name], 1)]

        block = ctx.enter_context(nc.Block())

        @block.sync
        def _(sp_):
            sp_.dma_start(par[:, :], par_in).then_inc(loaded, 16)
            for k in range(X_LOADS):
                part = slice(k * DC // X_LOADS, (k + 1) * DC // X_LOADS)
                sp_.dma_start(x[:, part, :], xT_in[:, part, :]).then_inc(x_loaded[k], 16)
                if k == 0:
                    sp_.dma_start(cst[:, :], cst_in).then_inc(loaded, 16)
            for s in range(RING):
                sp_.dma_start(ring[:, s, :], stream[s, :, :]).then_inc(w_ready[s], 16)
            sp_.dma_start(pT[:, :, :], pT_in).then_inc(p_loaded, 16)
            sp_.dma_start(posi[:, :], pos_in).then_inc(p_loaded, 16)
            with sp_.Fori(0, N_UNITS // RING - 1) as i:
                for s in range(RING):
                    sp_.wait_ge(unit_done, i * RING + (s + 1))
                    sp_.dma_start(ring[:, s, :], stream[bass.ds(i * RING + (RING + s), 1), :, :]
                                  .rearrange("a p n -> p (a n)")).then_inc(w_ready[s], 16)
            for u in range(N_UNITS // RING * RING, N_UNITS):
                sp_.wait_ge(unit_done, u - RING + 1)
                sp_.dma_start(ring[:, u % RING, :], stream[u, :, :]).then_inc(w_ready[u % RING], 16)
            sp_.wait_ge(unit_done, U_EXP)
            sp_.sem_inc(lo_done, RING)

            def store(q, i, k):
                sp_.wait_ge(gx_evac, q * BLOCKS + i * (2 * STORE) + (2 + STORE * (k + 1)))
                sp_.dma_start(dense[:, :, bass.ds(i * (2 * STORE * GB) + k * STORE * GB, STORE * GB)], stage[:, k, :, :])\
                    .then_inc(g_stored[k], 16)

            def u_group(q, i, early=None, late=None):
                for j in range(RING):
                    sp_.wait_ge(lo_done, q * E_Q + i * RING + (j + 1))
                    unit = u_in[bass.ds(q * E_A + i * RING + j, 1), :, :]
                    sp_.dma_start(ring[:, j, 0:D], unit.rearrange("a p n -> p (a n)")).then_inc(w_ready[j], 16)
                    if j == 1 and late is not None:
                        store(q, late, 1)
                    if j == 3 and early is not None:
                        store(q, early, 0)

            def v_unit(q, i, j, half):
                sp_.wait_ge(lo_done, q * E_Q + i * RING + (E_A + half * E_Y + j + 1))
                unit = v_in[bass.ds(q * (2 * E_Y) + i * RING + (half * E_Y + j), 1), :, :]
                sp_.dma_start(ring[:, j, 0:D], unit.rearrange("a p n -> p (a n)")).then_inc(w_ready[j], 16)

            def pair(q, i, j):
                sp_.wait_ge(mul_done, q * E_Y + i * G_SLOTS + (j + 1))
                sp_.dma_start(gw[:, j, :, :], dense[:, bass.ds(i * (2 * G_SLOTS) + 2 * j, 2), :]).then_inc(gw_ready[j], 16)

            def v_units(q):
                with sp_.Fori(1, E_Y // RING) as i:
                    for j in range(RING):
                        v_unit(q, i, j, 0)
                        pair(q, i, j)
                with sp_.Fori(0, E_Y // RING) as i:
                    for j in range(RING):
                        v_unit(q, i, j, 1)

            def stored(q):
                for k in range(2):
                    sp_.wait_ge(g_stored[k], q * (16 * B_GROUPS) + 16 * (B_GROUPS + 1))

            with sp_.Fori(0, E_A // RING) as i:
                u_group(0, i)
            for j in range(RING):
                v_unit(0, 0, j, 0)
            with sp_.Fori(0, B_GROUPS) as i:
                store(0, i, 0)
                store(0, i, 1)
            stored(0)
            for j in range(G_SLOTS):
                pair(0, 0, j)
            v_units(0)
            with sp_.Fori(1, NQ) as q:
                u_group(q, 0)
                u_group(q, 1, early=0)
                with sp_.Fori(2, B_GROUPS + 1) as i:
                    u_group(q, i, early=i - 1, late=i - 2)
                u_group(q, B_GROUPS + 1, late=B_GROUPS - 1)
                with sp_.Fori(B_GROUPS + 2, E_A // RING) as i:
                    u_group(q, i)
                stored(q)
                for j in range(G_SLOTS):
                    pair(q, 0, j)
                for j in range(RING):
                    v_unit(q, 0, j, 0)
                v_units(q)
            sp_.wait_ge(y_add, HB + NQ * DC)
            sp_.dma_start(out, x[:, :, :]).then_inc(out_done, 16)
            sp_.wait_ge(out_done, 16)

        @block.tensor
        def _(pe):
            def need(u, i=None, per=0):
                v = 16 * (u // RING + 1)
                if u < N_SPLIT:
                    pe.wait_ge(wt_low, u + 1 if i is None else i * per + (u + 1))
                pe.wait_ge(w_ready[u % RING], v if i is None else i * (16 * per // RING) + v)
                return ring[:, u % RING, :]

            def chunk(bank, w, rhs, k0=0, start=True, stop=True, kn=None):
                kn = rhs.shape[1] if kn is None else kn
                for k in range(kn):
                    m = pe.matmul(ps[:, bank, :], w[:, k * P:(k + 1) * P], rhs[:, k0 + k, :],
                                  start=start and k == 0, stop=stop and k == kn - 1)
                return m

            def split_products(bank, w, k0, kn, n, high, low, first, last, ready=None):
                for k in range(kn):
                    if ready is not None:
                        pe.wait_ge(hl_ready, ready + k + 1)
                    for part, rhs in ((0, high), (0, low), (1, high)):
                        m = pe.matmul(ps[:, bank, :], w[:, part, k0 + k * n:k0 + k * n + P], rhs(k),
                                      start=first and k == 0 and part == 0 and rhs is high,
                                      stop=last and k == kn - 1 and part == 1)
                return m

            def x_chunk(bank, u, i=None, per=0, ready=None, at=0):
                pe.wait_ge(wt_low, at + u + 1 if i is None else i * per + (u + 1))
                return split_products(bank, spl[:, u % 2, :, :], 0, DC, P, lambda k: hh[:, k, :], lambda k: hl[:, k, :],
                                      True, True, ready)

            def norm(n):
                sq = sq1 if n < 5 else sq2
                for c in range(NORMS[n]):
                    pe.wait_ge(sq_ready, NB[n] + c + 1)
                    m = pe.matmul(ps[:, 7, :], ones, sq[:, c, :], start=c == 0, stop=c == NORMS[n] - 1)
                m.then_inc(ss_ready, 1)

            def residual(u, passes, units):
                rhs = {U_OUT: merged, U_DOWN: act, U_OUT2: oall}[u]
                with pe.Fori(0, passes) as i:
                    for j in range(4 // units):
                        pe.wait_ge(x_add, i * (4 // units) + (X_BASE[u] + j + 1))
                        for h in range(units):
                            w = need(u + j * units + h, i, 4)
                            n = DC if units == 1 else FC // 2
                            chunk(3 + j, w, rhs, k0=h * (FC // 2), kn=n, start=h == 0, stop=h == units - 1)\
                                .then_inc(unit_done, 1)

            pe.wait_ge(loaded, 32)
            norm(0)
            with pe.Fori(0, HEADS_RG) as i:
                for k, (name, a) in enumerate(Z_ORDER):
                    if k == 6:
                        pe.wait_ge(xc_ready, i * 2 + 2)
                        for g in range(2):
                            w = need(RG_UNIT + g, i, 16)
                            for o in range(2):
                                pe.wait_ge(rg_evac, i * 4 + (2 * g + o + 1))
                                for kk in range(2):
                                    m = pe.matmul(ps[:, 7, :], w[:, (2 * kk + o) * P:(2 * kk + o + 1) * P],
                                                  xc[:, kk, :], start=kk == 0, stop=kk == 1)
                                m.then_inc(unit_done if o else rg_ready, 1)
                    pe.wait_ge(z_evac, i * 14 + (k + 1))
                    x_chunk(k % Z_BANKS, Z_UNIT[k], i, 16, 0 if k == 0 else None).then_inc(unit_done, 1)
            pe.wait_ge(chunk_done, 2 + DC)
            residual(U_OUT, 2, 1)
            norm(1)
            with pe.Fori(0, FC // 2) as i:
                for j in range(2):
                    pe.wait_ge(silu_done, i * 2 + (j + 1))
                    x_chunk(2 * j, U_FF + 2 * j, i, 4, DC if j == 0 else None).then_inc(unit_done, 1)
                    pe.wait_ge(ff_act, i * 2 + (j + 1))
                    x_chunk(2 * j + 1, U_FF + 2 * j + 1, i, 4).then_inc(unit_done, 1)
            pe.wait_ge(ff_act, 2 + FC)
            residual(U_DOWN, 4, 2)
            pe.wait_ge(silu_done, 2 + FC)
            pe.wait_ge(p_loaded, 32)
            pe.wait_ge(x_add, X_BASE[U_GATE])
            for g in range(2):
                w = need(U_PLE + g)
                for j in range(4):
                    if g:
                        pe.wait_ge(ple_evac, j + 1)
                    for kk in range(2):
                        m = pe.matmul(ps[:, j, :], w[:, (2 * j + kk) * P:(2 * j + kk + 1) * P], pT[:, kk, :],
                                      start=kk == 0, stop=kk == 1)
                m.then_inc(unit_done, 1)
            norm(2)
            for c in range(DC):
                if c < 4:
                    pe.wait_ge(ple_evac, 5 + c)
                else:
                    pe.wait_ge(gate_done, c - 3)
                x_chunk(c % 4, U_GATE + c, ready=2 * DC if c == 0 else None).then_inc(unit_done, 1)
            norm(3)
            norm(4)
            for c in range(14):
                if c >= 4:
                    pe.wait_ge(in_evac, c - 3)
                x_chunk(c % 4, U_IN2 + c, ready=3 * DC if c == 0 else None).then_inc(unit_done, 1)
            for h in range(2):
                pe.wait_ge(wt_low, U_TOK + h + 1)
                for t in range(TT):
                    for k in range(4):
                        for n, (rows, part) in enumerate(((hh, 0), (hh, 1), (hl, 0))):
                            m = pe.matmul(ps[:, 4 + t, 0:VW], rows[:, 4 * h + k, t * P:(t + 1) * P],
                                          spl[:, (U_TOK + h) % 2, part, k * VW:(k + 1) * VW],
                                          start=h == 0 and k == 0 and n == 0, stop=h == 1 and k == 3 and n == 2)
                m.then_inc(unit_done, 1)
            pe.wait_ge(in_evac, 14)
            for kv in range(2):
                pe.wait_ge(blk_ready, kv + 1)
                for m_ in range(2):
                    for h in range(2):
                        w = need(U_CMP + kv * 4 + m_ * 2 + h)
                        for j in range(8):
                            m = pe.matmul(ps[:, kv * 2 + m_, 0:A_G * N_CMP], w[:, j * P:(j + 1) * P],
                                          blk[:, kv, 8 * h + j, :], start=h == 0 and j == 0, stop=h == 1 and j == 7)
                        m.then_inc(unit_done, 1)
            w = need(U_CMP2)
            pe.wait_ge(tok_evac, 2 * TT)
            pe.wait_ge(hid_ready, 4)
            for m_ in range(2):
                pe.matmul(ps[:, 4, 0:A_G * N_CMP], w[:, m_ * P:(m_ + 1) * P], hid[:, 0, m_, :], start=m_ == 0, stop=m_ == 1)
            for g in range(A_G):
                for m_ in range(2):
                    m = pe.matmul(ps[0:N_CMP, 5, g * A_D:(g + 1) * A_D], hid[:, 1, m_, g * N_CMP:(g + 1) * N_CMP],
                                  w[:, 2 * P + m_ * A_D:2 * P + (m_ + 1) * A_D], start=m_ == 0, stop=m_ == 1)
            m.then_inc(unit_done, 1)
            norm(5)
            norm(6)
            pe.wait_ge(hn_ready, NB[7])
            for h in range(B_H):
                w = need(U_UQ + h // 4)
                if h >= 4:
                    pe.wait_ge(m_evac, h - 3)
                for k in range(2):
                    m = pe.matmul(ps[0:B_QK, h % 4, :], w[:, (k * 4 + h % 4) * B_QK:(k * 4 + h % 4 + 1) * B_QK], cq[:, k, :],
                                  start=k == 0, stop=k == 1)
                m.then_inc(unit_done if h % 4 == 3 else m_done, 1)
            w = need(U_UKV)
            for h in range(B_H):
                pe.wait_ge(m_evac, 5 + h)
                pe.matmul(ps[0:B_NOPE, h % 4, :], w[:, h * B_NOPE:(h + 1) * B_NOPE], cq[:, 2, :],
                          start=True, stop=True).then_inc(m_done, 1)
            pe.wait_ge(kc_evac, 2)
            for t in range(TT):
                if t >= 2:
                    pe.wait_ge(mv_evac, t - 1)
                m = pe.matmul(ps[:, 4 + t % 2, :], cq[:, 2, t * P:(t + 1) * P], w[:, 512:1024], start=True, stop=True)
                m.then_inc(unit_done if t == 3 else m_done, 1)
            pe.wait_ge(m_evac, 2 * B_H)

            def rope_items(i, base, per, rows, blk_c, rot_c, cols=T):
                n = [(i * 2 if i is not None else 0) + (base + j + 1) for j in range(per)]
                for j in range(per):
                    pe.wait_ge(rsq, n[j])
                    pe.matmul(ps[0:rows, j, 0:cols], blk_c, sqt[0:rows, j, 0:cols], start=True, stop=True).then_inc(rss, 1)
                for j in range(per):
                    pe.wait_ge(rxn, n[j])
                    pe.matmul(ps[0:rows, 2 + j, 0:cols], rot_c, xn[0:rows, j, 0:cols], start=True, stop=True).then_inc(rrot, 1)

            with pe.Fori(0, 3) as i:
                rope_items(i, 0, 2, P, cc("blk"), cc("rot_a"))
            rope_items(None, 6, 1, P, cc("blk"), cc("rot_a"), A_G * N_CMP)
            with pe.Fori(0, B_H) as i:
                rope_items(i, 7, 2, B_QK, cst[0:B_QK, 0:B_QK], cc("rot_b", B_QK))

            def attend(i, units, base):
                per = len(units)
                for s in range(per + 2):
                    if s < per:
                        g, kind, qt = units[s]
                        if s >= 3:
                            pe.wait_ge(at_exp, i * per + (base + s - 2))
                        bank, lo = s % 3, A_D * g
                        if kind == "mla":
                            nk = (qt + 1) * P
                            pe.matmul(ps[:, bank, 0:nk], q_cur[0:B_QK, g, qt * P:(qt + 1) * P], mqk[:, bass.ds(i * 2 + (B_H + g), 1), 0:nk].rearrange("p a t -> p (a t)"),
                                      start=True, stop=False)
                        elif kind == "cmp":
                            nk = N_CMP
                            pe.matmul(ps[:, bank, 0:nk], q_cur[lo:lo + A_D, 0, qt * P:(qt + 1) * P],
                                      kcn[lo:lo + A_D, 0, g * N_CMP:(g + 1) * N_CMP], start=True, stop=False)
                        else:
                            nk = (qt + 1) * P
                            pe.matmul(ps[:, bank, 0:nk], q_cur[lo:lo + A_D, 0, qt * P:(qt + 1) * P],
                                      qk[lo:lo + A_D, A_R + (kind == "win"), 0:nk], start=True, stop=False)
                        if kind == "cmp":
                            m = pe.matmul(ps[:, bank, 0:nk], identb[:, :], cmpb[:, qt, :], start=False, stop=True)
                        else:
                            m = pe.matmul(ps[:, bank, nk - P:nk], identb[:, :], causalb[:, :], start=False, stop=True)
                        m.then_inc(at_s, 1)
                    if s >= 2:
                        u = s - 2
                        g, kind, qt = units[u]
                        pe.wait_ge(at_scale, i * per + (base + u + 1))
                        if u >= 2:
                            pe.wait_ge(at_ev, i * per + (base + u - 1))
                        if kind == "cmp":
                            m = pe.transpose(ps[0:N_CMP, 3 + u % 2, 0:P], pr[:, u % 3, 0:N_CMP], cc("ident"))
                        else:
                            for kt in range(qt + 1):
                                m = pe.transpose(ps[:, 3 + u % 2, kt * P:(kt + 1) * P], pr[:, u % 3, kt * P:(kt + 1) * P],
                                                 cc("ident"))
                        m.then_inc(at_t, 1)
                    if s >= 3 and (s - 3) % TT == TT - 1:
                        output(i, units, s - 3, base)
                output(i, units, per - 1, base)

            def output(i, units, u, base):
                per = len(units)
                g, kind, _ = units[u]
                grp = u // TT
                pe.wait_ge(at_ev, i * per + (base + u + 1))
                lo = A_D * g
                first = kind in ("cmp", "mla")
                if kind == "cmp":
                    m = pe.matmul(ps[lo:lo + A_D, 5, :], vct[:, g, :], pt[0:N_CMP, grp % 2, 0, :], start=True, stop=False)
                else:
                    for kt in range(TT):
                        if kind == "mla":
                            v = v_cur[:, g, kt, :]
                        else:
                            c = (kind == "win") * P + lo
                            v = vtok[:, kt, c:c + A_D]
                        m = pe.matmul(ps[lo:lo + A_D, 5, kt * P:], v, pt[:, grp % 2, kt, kt * P:],
                                      start=first and kt == 0, stop=kt == TT - 1 and kind != "slc")
                m.then_inc(at_pv, 1)

            pe.wait_ge(rdone, 2 + 7 + 2 * B_H)
            with pe.Fori(0, A_R) as i:
                pe.wait_ge(cur_ready, i + 1)
                pe.wait_ge(at_out, i + 1)
                attend(i, NSA, S_NSA)
            with pe.Fori(0, B_H // 2) as i:
                pe.wait_ge(cur_ready, i * 4 + (A_R + 4))
                pe.wait_ge(at_out, i + (A_R + 1))
                attend(i, MLA, S_MLA)
            norm(7)
            norm(8)
            pe.wait_ge(hn_ready, NB[9])
            residual(U_OUT2, 2, 1)
            norm(9)
            for c in range(2 * E_H + 1):
                if c < 2 * E_H:
                    if c >= 4:
                        pe.wait_ge(qp_evac, 2 * (c - 3))
                    x_chunk(c % 4, c, ready=4 * DC if c == 0 else None, at=N_SPLIT).then_inc(unit_done, 1)
                if c:
                    pe.wait_ge(qp_evac, 2 * c)
                    for t in range(TT):
                        col = (c - 1) % 2 * TT * E_H + t * E_H + (c - 1) // 2
                        m = pe.matmul(ps[:, 6, col:col + 1], qs[:, (c - 1) % 4, t * P:(t + 1) * P], ones[:, 0:1],
                                      start=True, stop=True)
                    m.then_inc(qs_used, 1)
            need(U_KEYS)
            need(U_KEYS + 1)
            n = 0
            for t in range(TT):
                for b in range(4):
                    if n >= 4:
                        pe.wait_ge(sk_evac, 2 * (n - 3))
                    for j in range(4):
                        c = 4 * b + j
                        m = pe.matmul(ps[:, n % 4, j * P:(j + 1) * P], qp[:, c, t * P:(t + 1) * P],
                                      ring[:, (U_KEYS + c // 8) % RING, (c % 8) * P:(c % 8 + 1) * P], start=True, stop=True)
                    m.then_inc(sk_done, 1)
                    n += 1
            pe.wait_ge(sk_evac, 32)
            pe.sem_inc(unit_done, 2)
            def u_unit(q, i, j):
                pe.wait_ge(lo_done, q * E_Q + i * 4 + (RING + j + 1))
                pe.wait_ge(gelu_done, q * E_A + i * 4 + (j + 1))
                split_products(j, spl[:, j % 2, :, :], 0, DC, P, lambda k: hh[:, k, :], lambda k: hl[:, k, :],
                               True, True).then_inc(e_done, 1)

            def spread(q, i, j):
                pe.wait_ge(oh_ready, q * BLOCKS + i * (2 * STORE) + (j + 1))
                pe.wait_ge(gx_evac, q * BLOCKS + i * (2 * STORE) + (j + 1))
                for t in range(GB):
                    for k in range(3):
                        m = pe.matmul(ps[:, 4 + j % 2, t * QN:(t + 1) * QN], oh1[:, j % 2, :, t], oh2[:, j % 2, 1 + k, :, t],
                                      start=k == 0, stop=k == 2)
                m.then_inc(gx_done, 1)

            def experts_out(q):
                for half in range(2):
                    def unit(i, j, first, last):
                        e = q * E_Q + i * 4 + (E_A + half * E_Y + j)
                        pe.wait_ge(lo_done, e + (RING + 1))
                        pe.wait_ge(wl_ready, q * (2 * E_Y) + i * 4 + (half * E_Y + j + 1))
                        for c in range(HB):
                            if first:
                                pe.wait_ge(y_add, q * DC + (half * HB + c + 1))
                            for k in range(2):
                                m = split_products(4 + c, spl[:, j % 2, :, :], k * HB * P + c * P, 1, P,
                                                   lambda _: wsp[:, j % 2, 0, k * T:(k + 1) * T],
                                                   lambda _: wsp[:, j % 2, 1, k * T:(k + 1) * T],
                                                   first and k == 0, last and k == 1)
                            if last and c < HB - 1:
                                m.then_inc(y_part, 1)
                        m.then_inc(e_done, 1)
                    for j in range(4):
                        unit(0, j, j == 0, False)
                    with pe.Fori(1, E_Y // 4 - 1) as i:
                        for j in range(4):
                            unit(i, j, False, False)
                    for j in range(4):
                        unit(E_Y // 4 - 1, j, False, j == 3)

            with pe.Fori(0, E_A // 4) as i:
                for j in range(4):
                    u_unit(0, i, j)
            for t in range(TT):
                pe.wait_ge(sel_ready, t + 1)
                for k in range(3):
                    m = pe.transpose(ps[:, 4 + k, t * P:(t + 1) * P], sel[:, t, k, :], cc("ident"))
            m.then_inc(selt_done, 1)
            with pe.Fori(0, B_GROUPS) as i:
                for j in range(2 * STORE):
                    spread(0, i, j)
            pe.wait_ge(gx_evac, BLOCKS + 2)
            experts_out(0)
            with pe.Fori(1, NQ) as q:
                with pe.Fori(0, B_GROUPS) as i:
                    for j in range(4):
                        u_unit(q, i, j)
                        spread(q, i, 2 * j)
                        spread(q, i, 2 * j + 1)
                with pe.Fori(B_GROUPS, E_A // 4) as i:
                    for j in range(4):
                        u_unit(q, i, j)
                pe.wait_ge(gx_evac, q * BLOCKS + (BLOCKS + 2))
                experts_out(q)

        @block.scalar
        def _(eng):
            def highs(n):
                for c in range(DC):
                    eng.wait_ge(hn_ready, NB[n] + c + 1)
                    eng.activation(hh[:, c, :], hnt[:, c % 2, :], ACT.Copy).then_inc(hh_ready, 1)

            def squares(n, wait=None, src=x, at=0):
                sq = sq1 if n < 5 else sq2
                for c in range(NORMS[n]):
                    if n == 0 and c % (DC // X_LOADS) == 0:
                        eng.wait_ge(x_loaded[c * X_LOADS // DC], 16)
                    if wait is not None:
                        eng.wait_ge(wait[0], wait[1] + c + 1)
                    if n:
                        eng.wait_ge(ss_ready, n)
                    eng.activation(sq[:, c, :], src[:, at + c, :], ACT.Square).then_inc(sq_ready, 1)

            def rms(n, width=D):
                eng.wait_ge(ss_ready, n + 1)
                if n:
                    eng.wait_ge(hn_ready, NB[n])
                eng.activation(rstd[:, :], ps[:, 7, :], ACT.Sqrt, scale=1.0 / width, bias=pc("eps")).then_inc(rms_ready, 1)

            eng.wait_ge(loaded, 32)
            squares(0)
            eng.wait_ge(sp_abs, 1)
            eng.activation(sp[:, 1, :], sp[:, 0, :], ACT.Exp, scale=-1.0).then_inc(sp_exp, 1)
            rms(0)
            highs(0)
            eng.sem_inc(z_evac, Z_BANKS)
            eng.sem_inc(rg_evac, 1)
            eng.wait_ge(sp_ready, 2)

            def z(i, k, func, dst, **kw):
                eng.wait_ge(unit_done, i * 16 + (Z_UNIT[k] + 1))
                eng.activation(dst, ps[:, k % Z_BANKS, :], func, **kw).then_inc(z_evac, 1)

            with eng.Fori(0, HEADS_RG) as i:
                for k, (name, a) in enumerate(Z_ORDER):
                    if k == 6:
                        for g, (dst, b) in enumerate(((r_g, "b_r"), (i_g, "b_i"))):
                            for o in range(2):
                                if o:
                                    eng.wait_ge(unit_done, i * 16 + (RG_UNIT + g + 1))
                                else:
                                    eng.wait_ge(rg_ready, i * 2 + (g + 1))
                                eng.activation(dst[:, o, :], ps[:, 7, :], ACT.Sigmoid, bias=pd(b, i * 2 + o))\
                                    .then_inc(rg_evac, 1)
                        eng.wait_ge(rg_evac, i * 4 + 5)
                        for o in range(2):
                            eng.activation(th[:, o, :], r_g[:, o, :], ACT.Tanh, scale=sp[:, 4, bass.ds(i * 2 + o, 1)])\
                                .then_inc(th_ready, 1)
                        for o in range(2):
                            eng.activation(a_t[:, o, :], r_g[:, o, :], ACT.Exp, scale=sp[:, 5, bass.ds(i * 2 + o, 1)])\
                                .then_inc(a_ready, 1)
                        for o in range(2):
                            eng.wait_ge(m2_ready, i * 2 + (o + 1))
                            eng.activation(mlt[:, o, :], mlt[:, o, :], ACT.Sqrt, scale=2.0).then_inc(mlt_ready, 1)
                    if k < 2:
                        eng.wait_ge(chunk_done, i * 2 + (k + 1))
                        z(i, k, ACT.Copy, rxp[:, k, 3:])
                    elif name == "ry":
                        z(i, k, ACT.Gelu_apprx_tanh, zb["ry"][:, a, :])
                    elif name in ("gr", "gc"):
                        z(i, k, ACT.Sigmoid, zb[name][:, a, :])
                    else:
                        z(i, k, ACT.Copy, zb[name][:, a, :])
            eng.sem_inc(silu_done, 2)
            squares(1, (x_add, X_BASE[U_OUT] + 4))
            rms(1)
            highs(1)
            for k in range(4):
                eng.wait_ge(rope_ang, k + 1)
                eng.activation(rope[:, k, :], rope[:, k, :], ACT.Sin).then_inc(rope_ready, 1)
            with eng.Fori(0, FC // 2) as i:
                for j in range(2):
                    eng.wait_ge(unit_done, i * 4 + (U_FF + 2 * j + 1))
                    eng.wait_ge(ff_act, i * 2 + (j + 1))
                    eng.activation(sg[:, j, :], ps[:, 2 * j, :], ACT.Silu).then_inc(silu_done, 1)
            squares(2, (x_add, X_BASE[U_DOWN] + 2))
            for g in range(2):
                eng.wait_ge(unit_done, U_PLE + g + 1)
                for j in range(4):
                    eng.activation(pw[:, 4 * g + j, :], ps[:, j, :], ACT.Copy).then_inc(ple_evac, 1)
            rms(2)
            highs(2)
            for c in range(DC):
                eng.wait_ge(unit_done, U_GATE + c + 1)
                if c >= 2:
                    eng.wait_ge(x_add, X_BASE[U_GATE] + c - 1)
                eng.activation(gate[:, c % 2, :], ps[:, c % 4, :], ACT.Sigmoid).then_inc(gate_done, 1)
            squares(3, (x_add, X_BASE[U_GATE]))
            rms(3)
            squares(4, (hn_ready, NB[3]))
            rms(4)
            highs(4)
            for c in range(14):
                eng.wait_ge(unit_done, U_IN2 + c + 1)
                b = ps[:, c % 4, :]
                if c < 4 or c in (8, 9):
                    eng.activation(qk[:, c if c < 4 else c - 4, :], b, ACT.Copy).then_inc(in_evac, 1)
                elif c < 8:
                    eng.activation(kcd[0:A_D, c - 4, :], b[0:A_D, :], ACT.Copy)
                    eng.activation(kcd[A_D:, c - 4, 0:T - 1], b[A_D:, 1:T], ACT.Copy).then_inc(in_evac, 1)
                elif c < 13:
                    eng.activation(cq[:, c - 10, :], b, ACT.Copy).then_inc(in_evac, 1)
                else:
                    eng.activation(kr[B_NOPE:B_QK, :], b[B_NOPE:B_QK, :], ACT.Copy).then_inc(in_evac, 1)
            eng.wait_ge(unit_done, U_TOK + 2)
            for t in range(TT):
                eng.activation(vtok[:, t, 0:2 * P], ps[:, 4 + t, 0:2 * P], ACT.Copy).then_inc(tok_evac, 1)
            for t in range(TT):
                eng.activation(vtok[:, t, 2 * P:VW], ps[:, 4 + t, 2 * P:VW], ACT.Sigmoid).then_inc(tok_evac, 1)
            for kv in range(2):
                for m in range(2):
                    eng.wait_ge(unit_done, U_CMP + kv * 4 + m * 2 + 2)
                    eng.activation(hid[:, kv, m, :], ps[:, kv * 2 + m, 0:A_G * N_CMP], ACT.Gelu_apprx_tanh)\
                        .then_inc(hid_ready, 1)
            eng.wait_ge(unit_done, U_CMP2 + 1)
            eng.activation(kcn[:, 0, :], ps[:, 4, 0:A_G * N_CMP], ACT.Copy).then_inc(kc_evac, 1)
            eng.activation(vct[:, :, :].rearrange("p a d -> p (a d)"), ps[0:N_CMP, 5, 0:A_G * A_D], ACT.Copy)\
                .then_inc(kc_evac, 1)
            eng.wait_ge(in_evac, 14)
            squares(5, src=cq)
            rms(5, Q_LORA)
            squares(6, src=cq, at=2)
            rms(6, P)
            for h in range(B_H):
                if h % 4 == 3:
                    eng.wait_ge(unit_done, U_UQ + h // 4 + 1)
                else:
                    eng.wait_ge(m_done, h - h // 4 + 1)
                eng.activation(mqk[:, h, :], ps[0:B_QK, h % 4, :], ACT.Copy).then_inc(m_evac, 1)
            for h in range(B_H):
                eng.wait_ge(m_done, 6 + h + 1)
                eng.activation(mqk[0:B_NOPE, B_H + h, :], ps[0:B_NOPE, h % 4, :], ACT.Copy).then_inc(m_evac, 1)
            for t in range(TT):
                if t == 3:
                    eng.wait_ge(unit_done, U_UKV + 1)
                else:
                    eng.wait_ge(m_done, 14 + t + 1)
                eng.activation(vm[:, t, :], ps[:, 4 + t % 2, :], ACT.Copy).then_inc(mv_evac, 1)

            def rope_items(i, base, per, rows, src, width, cols=T):
                n = [(i * 2 if i is not None else 0) + (base + j + 1) for j in range(per)]
                for j in range(per):
                    at = bass.ds(i * 2 + j, 1) if i is not None else slice(0, 1)
                    eng.activation(sqt[0:rows, j, 0:cols], src[0:rows, at, 0:cols].rearrange("p a t -> p (a t)"),
                                   ACT.Square).then_inc(rsq, 1)
                for j in range(per):
                    eng.wait_ge(rss, n[j])
                    eng.wait_ge(rdone, n[j])
                    eng.activation(rst[0:rows, j, 0:cols], ps[0:rows, j, 0:cols], ACT.Sqrt, scale=1.0 / width,
                                   bias=par[0:rows, PAR["eps"]:PAR["eps"] + 1]).then_inc(rrms, 1)

            eng.wait_ge(m_evac, 2 * B_H)
            with eng.Fori(0, 3) as i:
                rope_items(i, 0, 2, P, qk, A_D)
            rope_items(None, 6, 1, P, kcn, A_D, A_G * N_CMP)
            eng.wait_ge(rope_ready, 5)
            with eng.Fori(0, B_H) as i:
                rope_items(i, 7, 2, B_QK, mqk, B_QK)
            eng.sem_inc(at_out, 1)

            def attend(i, units, base, pvbase):
                per, groups = len(units), len(units) // TT
                for s in range(per + 2):
                    if s < per:
                        g, kind, qt = units[s]
                        nk = N_CMP if kind == "cmp" else (qt + 1) * P
                        eng.wait_ge(at_max, i * per + (base + s + 1))
                        if s >= 3:
                            eng.wait_ge(at_t, i * per + (base + s - 2))
                        eng.activation(pr[:, s % 3, 0:nk], ps[:, s % 3, 0:nk], ACT.Exp, bias=st[:, s % 3, 0:1],
                                       accum_out=st[:, s % 3, 1:2]).then_inc(at_exp, 1)
                    if s >= 2:
                        u = s - 2
                        g, kind, qt = units[u]
                        grp = u // TT
                        eng.wait_ge(at_t, i * per + (base + u + 1))
                        if grp >= 2:
                            eng.wait_ge(at_pv, i * groups + (pvbase + grp - 1))
                        if kind == "cmp":
                            eng.activation(pt[0:N_CMP, grp % 2, 0, qt * P:(qt + 1) * P], ps[0:N_CMP, 3 + u % 2, 0:P],
                                           ACT.Copy).then_inc(at_ev, 1)
                        else:
                            eng.activation(pt[:, grp % 2, 0:qt + 1, qt * P:(qt + 1) * P],
                                           ps[:, 3 + u % 2, 0:(qt + 1) * P].rearrange("p (k q) -> p k q", q=P),
                                           ACT.Copy).then_inc(at_ev, 1)
                eng.wait_ge(at_pv, i * groups + (pvbase + groups))

            eng.wait_ge(rdone, 2 + 7)
            with eng.Fori(0, A_R) as i:
                eng.activation(q_cur[:, 0, :], qk[:, bass.ds(i, 1), :].rearrange("p a t -> p (a t)"), ACT.Copy)\
                    .then_inc(cur_ready, 1)
                attend(i, NSA, S_NSA, 0)
                eng.activation(oall[:, bass.ds(i, 1), :].rearrange("p a t -> p (a t)"), ps[:, 5, :], ACT.Copy)\
                    .then_inc(at_out, 1)
            eng.wait_ge(rdone, 2 + 7 + 2 * B_H)
            with eng.Fori(0, B_H // 2) as i:
                for h in range(2):
                    eng.activation(q_cur[0:B_QK, h, :], mqk[:, bass.ds(i * 2 + h, 1), :].rearrange("p a t -> p (a t)"),
                                   ACT.Copy).then_inc(cur_ready, 1)
                for h in range(2):
                    eng.activation(v_cur[:, h, :, :], vm[:, :, bass.ds(i * (2 * B_V) + h * B_V, B_V)], ACT.Copy)\
                        .then_inc(cur_ready, 1)
                attend(i, MLA, S_MLA, A_R * len(NSA) // TT)
                eng.activation(oall[:, bass.ds(i + A_R, 1), :].rearrange("p a t -> p (a t)"), ps[:, 5, :], ACT.Copy)\
                    .then_inc(at_out, 1)
            eng.wait_ge(at_out, 9)
            squares(7, src=oall)
            rms(7, A_H * A_D)
            squares(8, src=oall, at=4)
            rms(8, B_H * B_V)
            squares(9, (x_add, X_BASE[U_OUT2] + 4))
            rms(9)
            highs(9)
            for c in range(2 * E_H):
                eng.wait_ge(unit_done, U_WQ + c + 1)
                eng.activation(qp[:, c, :], ps[:, c % 4, :], ACT.Copy).then_inc(qp_evac, 1)
                if c >= 4:
                    eng.wait_ge(qs_used, c - 3)
                eng.activation(qs[:, c % 4, :], ps[:, c % 4, :], ACT.Square).then_inc(qp_evac, 1)
            eng.wait_ge(ssq_sum, 1)
            eng.activation(ssq[:, 0, :], ssq[:, 0, :], ACT.Sqrt, scale=1.0 / (2 * N_KEYS), bias=pc("eps"))\
                .then_inc(ssq_sqrt, 1)
            eng.wait_ge(rs_ready, 1)
            n = 0
            for t in range(TT):
                for b in range(4):
                    eng.wait_ge(sk_done, n + 1)
                    for j in range(2):
                        h = 2 * b + j
                        eng.activation(s_sb[:, t, 2 * h:2 * h + 2, :].rearrange("p a n -> p (a n)"),
                                       ps[:, n % 4, j * 256:(j + 1) * 256], ACT.Copy,
                                       scale=ssq[:, 0, t * E_H + h:t * E_H + h + 1]).then_inc(sk_evac, 1)
                    n += 1
            eng.wait_ge(sk_evac, 2 * 4 * TT)
            eng.sem_inc(gelu_done, 4)

            def weights(t):
                eng.wait_ge(tk_sub, t + 1)
                eng.activation(ce[:, :, :], ce[:, :, :], ACT.Exp).then_inc(tk_exp, 1)

            def high(e, j):
                eng.wait_ge(w_ready[j % RING], e * (16 // RING) + (16 * (U_EXP // RING + 1) - j % RING * (16 // RING)))
                eng.wait_ge(e_done, e + 1)
                eng.activation(spl[:, j % 2, 0, 0:D], ring[:, j % RING, 0:D], ACT.Copy).then_inc(hi_done, 1)

            def evacuate(q, i, j):
                if j % STORE == 0:
                    eng.wait_ge(g_stored[j // STORE], q * (16 * B_GROUPS) + i * 16 + 16)
                eng.wait_ge(gx_done, q * BLOCKS + i * (2 * STORE) + (2 + j + 1))
                eng.activation(stage[:, j // STORE, :, j % STORE * GB:(j % STORE + 1) * GB],
                               ps[:, 4 + j % 2, :].rearrange("p (t n) -> p n t", n=QN), ACT.Copy).then_inc(gx_evac, 1)

            def gelus(q, i0, i1, blocks=False):
                with eng.Fori(i0, i1) as i:
                    for j in range(4):
                        eng.wait_ge(e_done, q * E_Q + i * 4 + (2 + j + 1))
                        high(q * E_Q + i * 4 + (j + 2), j + 2)
                        eng.activation(gb[:, bass.ds(i * 4 + j, 1), :].rearrange("p a t -> p (a t)"), ps[:, j, :],
                                       ACT.Gelu_apprx_tanh).then_inc(gelu_done, 1)
                        if blocks:
                            evacuate(q, i, 2 * j)
                            evacuate(q, i, 2 * j + 1)

            def w_high(at, j, mul=None):
                if mul is not None:
                    eng.wait_ge(mul_done, mul + (G_SLOTS + 1))
                eng.activation(wsp[:, j % 2, 0, :], gb[:, at, :].rearrange("p a t -> p (a t)"), ACT.Copy)\
                    .then_inc(wh_ready, 1)

            def first_highs(q):
                for k in range(2):
                    eng.wait_ge(g_stored[k], q * (16 * B_GROUPS) + 16 * (B_GROUPS + 1))
                for j in range(2):
                    w_high(slice(2 * j, 2 * j + 2), j, q * E_Y + j)

            def outs(q, last):
                for half in range(2):
                    e0 = E_A + half * E_Y
                    with eng.Fori(0, E_Y // 4 - 1) as i:
                        for j in range(4):
                            eng.wait_ge(e_done, q * E_Q + i * 4 + (e0 + 2 + j + 1))
                            high(q * E_Q + i * 4 + (e0 + j + 2), j + 2)
                            w_high(bass.ds(i * 8 + (2 * (j + 2)), 2), j, q * E_Y + i * 4 + (j + 2) if half == 0 else None)
                    for j in range(4):
                        e = q * E_Q + (e0 + E_Y - 4 + j)
                        eng.wait_ge(e_done, e + 3)
                        if not (last and half == 1 and j >= 2):
                            high(e + 2, j + 2)
                        if j < 2:
                            w_high(slice(QN - 4 + 2 * j, QN - 2 + 2 * j), j, q * E_Y + (E_Y - 2 + j) if half == 0 else None)
                        elif half == 0:
                            w_high(slice(2 * j - 4, 2 * j - 2), j)

            eng.sem_inc(e_done, 2)
            for j in range(2):
                high(j, j)
            gelus(0, 0, 3)
            weights(0)
            gelus(0, 3, EARLY // 4)
            weights(1)
            eng.wait_ge(sel_ready, 2)
            gelus(0, EARLY // 4, E_A // 4)
            weights(2)
            weights(3)
            for k in range(2):
                eng.sem_inc(g_stored[k], 16)
            with eng.Fori(0, B_GROUPS) as i:
                for j in range(2 * STORE):
                    evacuate(0, i, j)
            first_highs(0)
            outs(0, False)

            def quarter(q, last):
                gelus(q, 0, B_GROUPS, True)
                gelus(q, B_GROUPS, E_A // 4 - 1)
                first_highs(q)
                gelus(q, E_A // 4 - 1, E_A // 4)
                outs(q, last)

            with eng.Fori(1, NQ - 1) as q:
                quarter(q, False)
            quarter(NQ - 1, True)

        @block.vector
        def _(dve):
            step = Order(dve, dve_order)

            def scale(n, g, dst, src=x, at=0, g_at=0):
                dve.wait_ge(rms_ready, n + 1)
                step(dve.reciprocal(rstd[:, :], rstd[:, :]))
                for c in range(NORMS[n]):
                    dve.scalar_tensor_tensor(out=dst[:, at + c, :], in0=src[:, at + c, :], scalar=pc(g, at=g_at + c),
                                             in1=rstd[:, :], op0=ALU.mult, op1=ALU.mult).then_inc(hn_ready, 1)

            def scale_parts(n, g):
                dve.wait_ge(rms_ready, n + 1)
                step(dve.reciprocal(rstd[:, :], rstd[:, :]))
                for c in range(DC + 1):
                    if c < DC:
                        if c >= 2:
                            dve.wait_ge(hl_ready, PARTED.index(n) * DC + c - 1)
                        dve.scalar_tensor_tensor(out=hnt[:, c % 2, :], in0=x[:, c, :], scalar=pc(g, at=c),
                                                 in1=rstd[:, :], op0=ALU.mult, op1=ALU.mult).then_inc(hn_ready, 1)
                    if c:
                        dve.wait_ge(hh_ready, PARTED.index(n) * DC + c)
                        dve.tensor_tensor(hl[:, c - 1, :], hnt[:, (c - 1) % 2, :], hh[:, c - 1, :].bitcast(F32),
                                          ALU.subtract).then_inc(hl_ready, 1)

            def fma(dst, a, w, b):
                step(dve.scalar_tensor_tensor(out=dst, in0=a, scalar=w, in1=b, op0=ALU.mult, op1=ALU.add))

            dve.wait_ge(loaded, 32)
            lam = pc("lam", DC)
            step(dve.tensor_scalar(sp[:, 2, :], lam, -1.0, None, ALU.mult))
            dve.tensor_tensor(sp[:, 0, :], lam, sp[:, 2, :], ALU.max).then_inc(sp_abs, 1)
            step(dve.tensor_scalar(sp[:, 2, :], sp[:, 2, :], 0.0, None, ALU.max))
            dve.wait_ge(sp_exp, 1)
            step(dve.tensor_scalar(sp[:, 3, :], sp[:, 1, :], 2.0, None, ALU.add))
            step(dve.reciprocal(sp[:, 3, :], sp[:, 3, :]))
            step(dve.tensor_tensor(sp[:, 3, :], sp[:, 1, :], sp[:, 3, :], ALU.mult))
            step(dve.tensor_tensor(sp[:, 4, :], sp[:, 3, :], sp[:, 3, :], ALU.mult))
            step(dve.memset(sp[:, 5, :], 2.0 / 17))
            for n in (15, 13, 11, 9, 7, 5, 3, 1):
                step(dve.tensor_tensor(sp[:, 5, :], sp[:, 5, :], sp[:, 4, :], ALU.mult))
                step(dve.tensor_scalar(sp[:, 5, :], sp[:, 5, :], 2.0 / n, None, ALU.add))
            step(dve.tensor_tensor(sp[:, 5, :], sp[:, 5, :], sp[:, 3, :], ALU.mult))
            step(dve.tensor_tensor(sp[:, 2, :], sp[:, 2, :], sp[:, 5, :], ALU.add))
            dve.tensor_scalar(sp[:, 4, :], sp[:, 2, :], RG_C, None, ALU.mult).then_inc(sp_ready, 1)
            dve.tensor_scalar(sp[:, 5, :], sp[:, 2, :], -RG_C, None, ALU.mult).then_inc(sp_ready, 1)
            step(dve.memset(rxp[:, :, 0:3], 0.0))
            step(dve.memset(prod[:, :, 0:2], 0.0))
            dve.sem_inc(chunk_done, 2)

            scale_parts(0, "g_mix")

            def z_is(i, k):
                dve.wait_ge(z_evac, i * 14 + (Z_BANKS + k + 1))

            def conv4(i, a):
                z_is(i, a)
                c = i * 2 + a
                step(dve.tensor_scalar(xc[:, a, :], rxp[:, a, 0:T], pd("conv4_w", c), pd("conv4_b", c), ALU.mult, ALU.add))
                for k in range(1, 3):
                    fma(xc[:, a, :], rxp[:, a, k:k + T], pd("conv4_w", c + k * DC), xc[:, a, :])
                dve.scalar_tensor_tensor(out=xc[:, a, :], in0=rxp[:, a, 3:3 + T], scalar=pd("conv4_w", c + 3 * DC),
                                         in1=xc[:, a, :], op0=ALU.mult, op1=ALU.add).then_inc(xc_ready, 1)

            def conv3(i, a):
                z_is(i, 5 if a == 0 else 11)
                c = i * 2 + a
                step(dve.tensor_tensor(prod[:, a, 2:], zb["cc"][:, a, :], zb["cx"][:, a, :], ALU.mult))
                step(dve.tensor_scalar(zb["cc"][:, a, :], prod[:, a, 0:T], pd("conv3_w", c), None, ALU.mult))
                fma(zb["cc"][:, a, :], prod[:, a, 1:1 + T], pd("conv3_w", c + DC), zb["cc"][:, a, :])
                fma(zb["cc"][:, a, :], prod[:, a, 2:2 + T], pd("conv3_w", c + 2 * DC), zb["cc"][:, a, :])
                step(dve.tensor_tensor(zb["cb"][:, a, :], zb["cb"][:, a, :], zb["cc"][:, a, :], ALU.mult))

            def join(i, a):
                z_is(i, 7 if a == 0 else 13)
                step(dve.tensor_tensor(hs[:, a, :], hs[:, a, :], zb["ry"][:, a, :], ALU.mult))
                step(dve.tensor_tensor(hs[:, a, :], hs[:, a, :], zb["gr"][:, a, :], ALU.mult))
                step(dve.tensor_tensor(zb["cb"][:, a, :], zb["cb"][:, a, :], zb["gc"][:, a, :], ALU.mult))
                dve.tensor_tensor(merged[:, bass.ds(i * 2 + a, 1), :].rearrange("p a t -> p (a t)"), hs[:, a, :],
                                  zb["cb"][:, a, :], ALU.add).then_inc(chunk_done, 1)

            with dve.Fori(0, HEADS_RG) as i:
                step.enter(i, 32)
                conv4(i, 0)
                conv4(i, 1)
                conv3(i, 0)
                for a in range(2):
                    dve.wait_ge(th_ready, i * 2 + (a + 1))
                    step(dve.tensor_scalar(mlt[:, a, :], th[:, a, :], 1.0, None, ALU.add))
                    step(dve.reciprocal(mlt[:, a, :], mlt[:, a, :]))
                    dve.tensor_tensor(mlt[:, a, :], mlt[:, a, :], th[:, a, :], ALU.mult).then_inc(m2_ready, 1)
                dve.wait_ge(rg_evac, i * 4 + 5)
                dve.wait_ge(xc_ready, i * 2 + 2)
                for a in range(2):
                    step(dve.tensor_tensor(i_g[:, a, :], i_g[:, a, :], xc[:, a, :], ALU.mult))
                for a in range(2):
                    dve.wait_ge(mlt_ready, i * 2 + (a + 1))
                    dve.wait_ge(a_ready, i * 2 + (a + 1))
                    step(dve.tensor_tensor(i_g[:, a, :], i_g[:, a, :], mlt[:, a, :], ALU.mult))
                    step(dve.tensor_tensor_scan(out=hs[:, a, :], data0=a_t[:, a, :], data1=i_g[:, a, :], initial=0.0,
                                                op0=ALU.mult, op1=ALU.add))
                join(i, 0)
                conv3(i, 1)
                join(i, 1)
                step.leave(HEADS_RG)

            def residual(u, passes, units):
                with dve.Fori(0, passes) as i:
                    for j in range(4 // units):
                        dve.wait_ge(unit_done, i * 4 + (u + (j + 1) * units))
                        xs = x[:, bass.ds(i * (4 // units) + j, 1), :].rearrange("p a t -> p (a t)")
                        dve.tensor_tensor(xs, xs, ps[:, 3 + j, :], ALU.add).then_inc(x_add, 1)

            dve.sem_inc(x_add, 4)
            residual(U_OUT, 2, 1)
            dve.sem_inc(ff_act, 2)
            scale_parts(1, "g_ffn")
            dve.wait_ge(p_loaded, 32)
            step(dve.tensor_copy(ang[:, 2, :], posi[:, :]))
            for t, inv in enumerate(("inv_a", "inv_b")):
                a, k = ang[:, 0, :], ang[:, 1, :]
                step(dve.tensor_scalar(a, ang[:, 2, :], cc(inv), None, ALU.mult))
                step(dve.tensor_scalar(k, a, 1 / TWO_PI, ROUND, ALU.mult, ALU.add))
                step(dve.tensor_scalar(k, k, -ROUND, None, ALU.add))
                for part in TWO_PI_PARTS:
                    step(dve.scalar_tensor_tensor(out=a, in0=k, scalar=-part, in1=a, op0=ALU.mult, op1=ALU.add))
                step(dve.tensor_scalar(k, a, TWO_PI / 4, -TWO_PI, ALU.is_gt, ALU.mult))
                step(dve.scalar_tensor_tensor(out=k, in0=a, scalar=TWO_PI / 4, in1=k, op0=ALU.add, op1=ALU.add))
                dve.tensor_scalar(rope[:, 2 * t, :], k, PI_BELOW, -PI_BELOW, ALU.min, ALU.max).then_inc(rope_ang, 1)
                dve.tensor_scalar(rope[:, 2 * t + 1, :], a, PI_BELOW, -PI_BELOW, ALU.min, ALU.max).then_inc(rope_ang, 1)
                dve.wait_ge(rope_ang, 2 * t + 2)
            with dve.Fori(0, FC // 2) as i:
                for j in range(2):
                    dve.wait_ge(unit_done, i * 4 + (U_FF + 2 * j + 2))
                    dve.wait_ge(silu_done, i * 2 + (2 + j + 1))
                    dve.tensor_tensor(act[:, bass.ds(i * 2 + j, 1), :].rearrange("p a t -> p (a t)"), sg[:, j, :],
                                      ps[:, 2 * j + 1, :], ALU.mult).then_inc(ff_act, 1)
            dve.sem_inc(x_add, 2)
            residual(U_DOWN, 4, 2)
            scale_parts(2, "g_ple")
            dve.wait_ge(ple_evac, DC)
            for c in range(DC):
                dve.wait_ge(gate_done, c + 1)
                step(dve.tensor_tensor(gate[:, c % 2, :], gate[:, c % 2, :], pw[:, c, :], ALU.mult))
                dve.tensor_tensor(x[:, c, :], x[:, c, :], gate[:, c % 2, :], ALU.add).then_inc(x_add, 1)
            dve.wait_ge(x_add, X_BASE[U_GATE] + DC)
            scale(3, "g_final", x)
            scale_parts(4, "norm1")
            step(dve.tensor_scalar(pc("qk_gain", A_R), pc("qk_gain", A_R), A_D ** -0.5, None, ALU.mult))
            step(dve.tensor_scalar(pc("mla_gain", B_H), pc("mla_gain", B_H), B_QK ** -0.5, None, ALU.mult))
            step(dve.tensor_copy(identb[:, :], cc("ident")))
            step(dve.tensor_copy(causalb[:, :], cc("causal")))
            step(dve.tensor_copy(cmpb[:, :, :].rearrange("p a n -> p (a n)"), cc("cmp_mask")))
            for kv in range(2):
                dve.wait_ge(in_evac, 6 + 2 * kv)
                for j in range(CMP_LEN // 2):
                    o = dve.tensor_scalar(blk[:, kv, j, :].rearrange("p (g n) -> p g n", g=A_G),
                                          kcd[:, 2 * kv:2 * kv + 2, 2 * j:2 * j + (N_CMP - 1) * CMP_STRIDE + 1:CMP_STRIDE],
                                          pc("pos_w", at=j), None, ALU.add)
                o.then_inc(blk_ready, 1)
            scale(5, "lora_q", cq, src=cq)
            scale(6, "lora_kv", cq, src=cq, at=2)
            dve.wait_ge(in_evac, 14)
            dve.tensor_copy(mqk[B_NOPE:B_QK, B_H:, :],
                            kr[B_NOPE:B_QK, :].unsqueeze(1).to_broadcast([B_ROPE, B_H, T])).then_inc(rope_ready, 1)
            dve.wait_ge(rope_ready, 5)

            def rope_items(i, base, per, rows, src, gain, table, cols=T, sub=None):
                n = [(i * 2 if i is not None else 0) + (base + j + 1) for j in range(per)]
                at = [bass.ds(i * 2 + j, 1) if i is not None else slice(0, 1) for j in range(per)]
                v = [src[0:rows, at[j], 0:cols].rearrange("p a t -> p (a t)") for j in range(per)]
                cos, sin = (rope[0:rows, table + k, :] for k in range(2))

                def by(dst, a, tab):
                    if sub is None:
                        return dve.tensor_tensor(dst, a, tab, ALU.mult)
                    tab = tab[:, CMP_LEN - 1::CMP_STRIDE].unsqueeze(1).to_broadcast([rows, A_G, N_CMP])
                    two_d = lambda z: z.rearrange("p (g n) -> p g n", g=A_G)
                    return dve.tensor_tensor(two_d(dst), two_d(a), tab, ALU.mult)

                for j in range(per):
                    g = par[0:rows, bass.ds(i * 2 + (PAR[gain] + j), 1)] if i is not None \
                        else par[0:rows, PAR[gain]:PAR[gain] + 1]
                    dve.wait_ge(rrms, n[j])
                    step(dve.reciprocal(rst[0:rows, j, 0:cols], rst[0:rows, j, 0:cols]))
                    dve.scalar_tensor_tensor(out=xn[0:rows, j, 0:cols], in0=v[j], scalar=g, in1=rst[0:rows, j, 0:cols],
                                             op0=ALU.mult, op1=ALU.mult).then_inc(rxn, 1)
                for j in range(per):
                    dve.wait_ge(rrot, n[j])
                    step(by(rt[0:rows, j, 0:cols], ps[0:rows, 2 + j, 0:cols], sin))
                    dve.wait_ge(rxn, n[j])
                    step(by(xn[0:rows, j, 0:cols], xn[0:rows, j, 0:cols], cos))
                    dve.tensor_tensor(v[j], xn[0:rows, j, 0:cols], rt[0:rows, j, 0:cols], ALU.add).then_inc(rdone, 1)

            dve.sem_inc(rdone, 2)
            with dve.Fori(0, 3) as i:
                step.enter(i, 6)
                rope_items(i, 0, 2, P, qk, "qk_gain", 0)
                step.leave(3)
            rope_items(None, 6, 1, P, kcn, "kc_gain", 0, A_G * N_CMP, True)
            with dve.Fori(0, B_H) as i:
                step.enter(i, 6)
                rope_items(i, 7, 2, B_QK, mqk, "mla_gain", 2)
                step.leave(B_H)

            def attend(i, units, base):
                per = len(units)
                for s in range(per + 1):
                    if s < per:
                        g, kind, qt = units[s]
                        nk = N_CMP if kind == "cmp" else (qt + 1) * P
                        dve.wait_ge(at_s, i * per + (base + s + 1))
                        dve.tensor_reduce(st[:, s % 3, 0:1], ps[:, s % 3, 0:nk], AX_X, ALU.max, negate=True)\
                            .then_inc(at_max, 1)
                    if s >= 1:
                        u = s - 1
                        g, kind, qt = units[u]
                        nk = N_CMP if kind == "cmp" else (qt + 1) * P
                        p_ = pr[:, u % 3, 0:nk]
                        dve.wait_ge(at_exp, i * per + (base + u + 1))
                        step(dve.reciprocal(st[:, u % 3, 2:3], st[:, u % 3, 1:2]))
                        if kind == "cmp" and qt == 0:
                            step(dve.tensor_tensor(p_, p_, cc("cmp_seen"), ALU.mult))
                        if kind == "mla":
                            o = dve.tensor_scalar(p_, p_, st[:, u % 3, 2:3], None, ALU.mult)
                        else:
                            col = 2 * P + g * A_R * 3 + ("cmp", "slc", "win").index(kind)
                            o = dve.tensor_scalar(p_, p_, st[:, u % 3, 2:3],
                                                  vtok[:, qt, bass.ds(i * 3 + col, 1)], ALU.mult, ALU.mult)
                        o.then_inc(at_scale, 1)

            dve.wait_ge(tok_evac, 2 * TT)
            with dve.Fori(0, A_R) as i:
                step.enter(i, len(NSA) + 2)
                attend(i, NSA, S_NSA)
                step.leave(A_R)
            with dve.Fori(0, B_H // 2) as i:
                step.enter(i, len(MLA))
                attend(i, MLA, S_MLA)
                step.leave(B_H // 2)
            scale(7, "out_gain", oall, src=oall)
            scale(8, "out_gain", oall, src=oall, at=4, g_at=4)
            dve.sem_inc(x_add, 4)
            residual(U_OUT2, 2, 1)
            scale_parts(9, "norm2")
            dve.wait_ge(qs_used, 2 * E_H)
            step(dve.tensor_copy(ssq[:, :, :].rearrange("p a n -> p (a n)"), ps[:, 6, 0:2 * TT * E_H]))
            dve.tensor_tensor(ssq[:, 0, :], ssq[:, 0, :], ssq[:, 1, :], ALU.add).then_inc(ssq_sum, 1)
            dve.wait_ge(ssq_sqrt, 1)
            dve.reciprocal(ssq[:, 0, :], ssq[:, 0, :]).then_inc(rs_ready, 1)

            def top16(lists):
                for half in range(2):
                    part = slice(8 * half, 8 * half + 8)
                    if half:
                        for vals, idx, src in lists:
                            o = dve.match_replace(src, vals[:, 0:8], src, NEG_HUGE)
                        step(o)
                    for vals, idx, src in lists:
                        o = dve.max(vals[:, part], src)
                    step(o)
                    for vals, idx, src in lists:
                        o = dve.max_index(idx[:, part], vals[:, part], src)
                    step(o)

            bc = [P, E_H, E_K, E_K]
            flat = lambda z: z.rearrange("p a b c -> p (a b c)")
            step(dve.tensor_copy(places[:, :], cc("iota16")))
            for i in range(TT):
                dve.wait_ge(sk_evac, i * 8 + 8)
                top16([(tv[:, k, h, :], ti[:, k, h, :], s_sb[:, i, 2 * h + k, :]) for h in range(E_H) for k in range(2)])
                step(dve.tensor_tensor(cand[:, :, :, :], tv[:, 0, :, :].unsqueeze(3).to_broadcast(bc),
                                       tv[:, 1, :, :].unsqueeze(2).to_broadcast(bc), ALU.add))
                top16([(cv[:, h, :], ci[:, h, :], cand[:, h, :, :].rearrange("p a b -> p (a b)")) for h in range(E_H)])
                dve.tensor_tensor(ce[:, :, :], cv[:, :, :], cv[:, :, 0:1].to_broadcast([P, E_H, E_K]), ALU.subtract)\
                    .then_inc(tk_sub, 1)
                step(dve.tensor_copy(flat(tif[:, :, :, :]), flat(ti[:, :, :, :])))
                step(dve.tensor_scalar(cm[:, 0, :, :], ci[:, :, :], 4, None, ALU.logical_shift_right))
                step(dve.tensor_scalar(cm[:, 1, :, :], ci[:, :, :], 15, None, ALU.bitwise_and))
                step(dve.tensor_copy(flat(cmf[:, :, :, :]), flat(cm[:, :, :, :])))
                for k in range(2):
                    step(dve.tensor_tensor(oh[:, :, :, :], cmf[:, k, :, :].unsqueeze(3).to_broadcast(bc),
                                           places[:, :].unsqueeze(1).unsqueeze(1).to_broadcast(bc), ALU.is_equal))
                    step(dve.tensor_tensor(oh[:, :, :, :], oh[:, :, :, :],
                                           tif[:, k, :, :].unsqueeze(2).to_broadcast(bc), ALU.mult))
                    step(dve.tensor_reduce(sel[:, i:i + 1, k, :].rearrange("p a (h k) -> p (a h) k", h=E_H),
                                           oh[:, :, :, :], AX_X, ALU.add))
                dve.wait_ge(tk_exp, i + 1)
                step(dve.tensor_reduce(gs[:, 0, :], ce[:, :, :], AX_X, ALU.add))
                step(dve.reciprocal(gs[:, 1, :], gs[:, 0, :]))
                dve.tensor_tensor(sel[:, i:i + 1, 2, :].rearrange("p a (h k) -> p (a h) k", h=E_H), ce[:, :, :],
                                  gs[:, 1, :].unsqueeze(2).to_broadcast([P, E_H, E_K]), ALU.mult).then_inc(sel_ready, 1)
                dve.wait_ge(sel_ready, i + 1)
            dve.wait_ge(selt_done, 1)
            step(dve.tensor_copy(n1t[:, :], ps[:, 4, :]))
            step(dve.tensor_copy(n2q[:, :], ps[:, 5, :]))
            step(dve.tensor_copy(g3[:, 0, :], ps[:, 6, :]))
            step(dve.tensor_tensor(gf[:, 0, :], ps[:, 6, :], g3[:, 0, :], ALU.subtract))
            step(dve.tensor_copy(g3[:, 1, :], gf[:, 0, :]))
            step(dve.tensor_tensor(gf[:, 1, :], gf[:, 0, :], g3[:, 1, :], ALU.subtract))
            step(dve.tensor_copy(g3[:, 2, :], gf[:, 1, :]))
            dve.sem_inc(gx_done, 2)
            dve.sem_inc(gx_evac, 2)
            dve.sem_inc(y_add, HB)
            dve.sem_inc(mul_done, G_SLOTS)
            dve.wait_ge(iota_ready, 1)
            with dve.Fori(0, NQ) as q:
                with dve.Fori(0, BLOCKS // 2) as b:
                    for j in range(2):
                        tok = bass.ds(b * (2 * GB) + j * GB, GB)
                        dve.wait_ge(gx_done, q * BLOCKS + (b * 2 + (j + 1)))
                        dve.tensor_tensor(oh2[:, j, 0, :, :], n2q[:, tok].unsqueeze(1).to_broadcast([P, QN, GB]),
                                          iota[:, 0:QN, :], ALU.is_equal).then_inc(oh_eq, 1)
                        dve.tensor_tensor(oh1[:, j, :, :], n1t[:, tok].unsqueeze(1).to_broadcast([P, N_KEYS, GB]),
                                          iota[:, :, :], ALU.is_equal)
                        dve.wait_ge(oh_eq, q * BLOCKS + (b * 2 + (j + 1)))
                        dve.tensor_tensor(oh2[:, j, 1:4, :, :], oh2[:, j, 0:1, :, :].to_broadcast([P, 3, QN, GB]),
                                          g3[:, :, tok].unsqueeze(2).to_broadcast([P, 3, QN, GB]), ALU.mult)\
                            .then_inc(oh_ready, 1)
                dve.wait_ge(oh_ready, q * BLOCKS + BLOCKS)
                dve.tensor_scalar(n2q[:, :], n2q[:, :], -float(QN), None, ALU.add).then_inc(n2_next, 1)
                dve.wait_ge(n2_next, q + 1)

                def weigh(i, j):
                    g = gb[:, bass.ds(i * 8 + 2 * j, 2), :]
                    dve.wait_ge(gelu_done, q * E_A + i * 8 + (2 * j + 2 + 4))
                    dve.wait_ge(gw_ready[j], q * (16 * E_Y // G_SLOTS) + i * 16 + 16)
                    dve.tensor_tensor(g, g, gw[:, j, :, :], ALU.mult).then_inc(mul_done, 1)

                def low(i, j, half):
                    dve.wait_ge(wh_ready, q * (2 * E_Y) + i * 4 + (half * E_Y + j + 1))
                    dve.tensor_tensor(wsp[:, j % 2, 1, :],
                                      gb[:, bass.ds(i * 8 + 2 * j, 2), :].rearrange("p a t -> p (a t)"),
                                      wsp[:, j % 2, 0, :].bitcast(F32), ALU.subtract).then_inc(wl_ready, 1)

                for half in range(2):
                    if half == 0:
                        weigh(0, 0)
                        weigh(0, 1)
                    with dve.Fori(0, E_Y // 4 - 1) as i:
                        for j in range(4):
                            if half == 0:
                                weigh(i if j < 2 else i + 1, (j + 2) % 4)
                            low(i, j, half)
                    for j in range(4):
                        if half == 0 and j < 2:
                            weigh(E_Y // 4 - 1, j + 2)
                        low(E_Y // 4 - 1, j, half)
                    for c in range(HB):
                        if c < HB - 1:
                            dve.wait_ge(y_part, q * (2 * (HB - 1)) + (half * (HB - 1) + c + 1))
                        else:
                            dve.wait_ge(e_done, q * E_Q + (2 + E_A + (half + 1) * E_Y))
                        xs = x[:, half * HB + c, :]
                        dve.tensor_tensor(xs, xs, ps[:, 4 + c, :], ALU.add).then_inc(y_add, 1)

        @block.gpsimd
        def _(pool):
            pool.iota(iota[:, :, :], pattern=[[1, N_KEYS], [0, GB]], base=0, channel_multiplier=0,
                      allow_small_or_imprecise_dtypes=True).then_inc(iota_ready, 1)
            def unit_parts(j, count, n=D):
                pool.tensor_tensor(spl[:, j % 2, 0, 0:n], ring[:, j, 0:n], zero[:, :].to_broadcast([P, n]), ALU.add)\
                    .then_inc(wt_high, 1)
                pool.wait_ge(wt_high, count)
                pool.tensor_tensor(spl[:, j % 2, 1, 0:n], ring[:, j, 0:n], spl[:, j % 2, 0, 0:n].bitcast(F32), ALU.subtract)\
                    .then_inc(wt_low, 1)

            pool.memset(zero[:, :], 0.0).then_inc(zero_ready, 1)
            pool.wait_ge(zero_ready, 1)
            for j in range(RING):
                pool.wait_ge(w_ready[j], 16)
                if j >= 2:
                    pool.wait_ge(unit_done, j - 1)
                unit_parts(j, j + 1)
            with pool.Fori(1, U_TOK // RING) as i:
                for j in range(RING):
                    pool.wait_ge(w_ready[j], i * 16 + 16)
                    pool.wait_ge(unit_done, i * RING + (j - 1))
                    unit_parts(j, i * RING + (j + 1))
            for u in range(U_TOK, N_SPLIT):
                pool.wait_ge(w_ready[u % RING], 16 * (u // RING + 1))
                pool.wait_ge(unit_done, u - 1)
                unit_parts(u % RING, u + 1, 4 * VW)
            for c in range(2 * E_H):
                u = U_WQ + c
                pool.wait_ge(w_ready[u % RING], 16 * (u // RING + 1))
                pool.wait_ge(unit_done, u - 1 if c >= 2 else N_SPLIT)
                unit_parts(u % RING, N_SPLIT + c + 1)
            with pool.Fori(0, NQ * E_Q // RING) as i:
                for j in range(RING):
                    pool.wait_ge(hi_done, i * RING + (j + 1))
                    pool.tensor_tensor(spl[:, j % 2, 1, 0:D], ring[:, j, 0:D], spl[:, j % 2, 0, 0:D].bitcast(F32),
                                       ALU.subtract).then_inc(lo_done, 1)


S_NSA = 0
S_MLA = A_R * A_G * 3 * TT
TWO_PI = 6.283185307179586
TWO_PI_PARTS = (6.28125, 0.00193500518798828125, 3.0199159819e-7)
ROUND = 12582912.0
PI_BELOW = 3.1415925
X_BASE = {U_OUT: 0, U_DOWN: 4 + DC, U_GATE: 4 + DC + 2 + DC, U_OUT2: 4 + DC + 2 + DC + DC}


def _feature_major(a):
    return np.ascontiguousarray(a.T.reshape(-1, P, a.shape[0]).transpose(1, 0, 2))


def _unit(w):
    u = w.reshape(-1, P, w.shape[1]).transpose(1, 0, 2).reshape(P, -1)
    return np.pad(u, ((0, 0), (0, UNIT - u.shape[1])))


def _chan(v):
    return v.reshape(-1, P).T


def _cat(ws):
    u = np.concatenate([w.reshape(-1, P, w.shape[1]).transpose(1, 0, 2).reshape(P, -1) for w in ws], 1)
    return np.pad(u, ((0, 0), (0, UNIT - u.shape[1])))


def _by_r(w):
    return w.reshape(A_G, A_R, A_D, -1).transpose(1, 0, 2, 3).reshape(A_H * A_D, -1)


def _rotation(width, blocks, half):
    m = np.zeros((P, width), np.float32)
    for b in blocks:
        for i in range(half):
            m[b + half + i, b + i] = -1.0
            m[b + i, b + half + i] = 1.0
    return m


def _constants():
    c = np.zeros((P, N_CST), np.float32)
    put = lambda name, v: c.__setitem__((slice(None), slice(*CST[name])), v)
    row = np.arange(P)
    put("ones", 1.0)
    put("ident", np.eye(P))
    put("blk", (row[:, None] // A_D == row[None] // A_D))
    put("rot_a", _rotation(P, (0, A_D), A_ROT // 2))
    put("rot_b", _rotation(B_QK, (B_NOPE,), B_ROPE // 2))
    put("causal", np.where(row[None] <= row[:, None], 0.0, MASKED))
    tok = np.arange(TT)[None, :, None] * P + row[:, None, None]
    end = np.arange(N_CMP)[None, None] * CMP_STRIDE + CMP_LEN - 1
    put("cmp_mask", np.where(end <= tok, 0.0, MASKED).reshape(P, -1))
    put("cmp_seen", (end <= tok)[:, 0])
    inv = lambda n: np.float32(ROPE_THETA) ** (-np.arange(0, n, 2, dtype=np.float32) / n)
    a = np.zeros(P, np.float32)
    b = np.zeros(P, np.float32)
    for base in (0, A_D):
        a[base:base + A_ROT] = np.tile(inv(A_ROT), 2)
    b[B_NOPE:B_QK] = np.tile(inv(B_ROPE), 2)
    put("inv_a", a[:, None])
    put("inv_b", b[:, None])
    put("iota16", np.arange(E_K)[None])
    return c


def _stream(n):
    units = []
    w_in = n["w_in"][0]
    for h in range(HEADS_RG):
        us = {}
        for k, (name, a) in enumerate(Z_ORDER):
            c = Z_SPLIT[name] * D + (2 * h + a) * P
            us[Z_UNIT[k]] = _unit(w_in[:, c:c + P])
        for g, name in enumerate(("w_rg_r", "w_rg_i")):
            us[RG_UNIT + g] = _unit(n[name][0, h])
        units += [us[k] for k in range(16)]
    cols = lambda w: [_unit(w[:, c * P:(c + 1) * P]) for c in range(w.shape[1] // P)]
    units += cols(n["w_out"][0])
    gu = cols(n["w_gate_up"][0])
    for c in range(FC):
        units += [gu[c], gu[FC + c]]
    wd = n["w_down"][0]
    for c in range(DC):
        for h in range(2):
            units.append(_unit(wd[h * FF // 2:(h + 1) * FF // 2, c * P:(c + 1) * P]))
    wp = n["w_ple"][0]
    for g in range(2):
        w = wp[:, g * 4 * P:(g + 1) * 4 * P].reshape(2, P, 4, P).transpose(1, 2, 0, 3).reshape(P, -1)
        units.append(np.pad(w, ((0, 0), (0, UNIT - w.shape[1]))))
    units += cols(n["w_ple_gate"][0])
    w2 = n["w_in_2"][0]
    at = np.cumsum((0, 512, 128, 128, 128, 128, 128, 128, 24, Q_LORA, 128, B_ROPE))
    q, kc, vc, ks, vs, kw, vw, gt, cq, ckv, krw = (w2[:, at[k]:at[k + 1]] for k in range(11))
    for r in range(A_R):
        units.append(_unit(np.concatenate([q[:, (g * A_R + r) * A_D:(g * A_R + r + 1) * A_D] for g in range(A_G)], 1)))
    for w in (kc, vc):
        for g in range(A_G):
            units.append(_unit(np.concatenate([w[:, g * A_D:(g + 1) * A_D]] * 2, 1)))
    units += [_unit(ks), _unit(kw), _unit(cq[:, :P]), _unit(cq[:, P:]), _unit(ckv),
              _unit(np.pad(krw, ((0, 0), (B_NOPE, P - B_QK))))]
    tok = np.concatenate([vs, vw, gt], 1)
    units += [_unit(tok[:D // 2]), _unit(tok[D // 2:])]
    for w in (n["cmp_k_w1_2"][0], n["cmp_v_w1_2"][0]):
        for m in range(2):
            for h in range(2):
                units.append(_unit(w[h * 1024:(h + 1) * 1024, m * P:(m + 1) * P]))
    k2, v2 = n["cmp_k_w2_2"][0], n["cmp_v_w2_2"][0]
    units.append(_cat([np.concatenate([k2, k2], 1), v2]))
    uq = n["mla_w_uq_2"][0]
    units += [_unit(uq[:, :4 * B_QK]), _unit(uq[:, 4 * B_QK:])]
    ukv = n["mla_w_ukv_2"][0].reshape(P, B_H, B_NOPE + B_V)
    units.append(_unit(np.concatenate([ukv[:, :, :B_NOPE].reshape(P, -1), ukv[:, :, B_NOPE:].reshape(P, -1)], 1)))
    wo = n["w_out_2"][0]
    units += cols(np.concatenate([_by_r(wo[:A_H * A_D]), wo[A_H * A_D:]]))
    units += cols(n["peer_w_q_2"][0])
    keys = n["peer_sub_keys_2"][0].reshape(2 * E_H, N_KEYS, N_KEYS).transpose(2, 0, 1)
    units += [_unit(keys[:, :E_H].reshape(P, -1)), _unit(keys[:, E_H:].reshape(P, -1))]
    assert len(units) == N_UNITS
    return np.stack(units)


def _twice(v):
    return np.concatenate([v, v])[:, None]


def _rows(v):
    return np.pad(v, (0, P - v.size))[:, None]


def kernel(**inputs):
    import concourse.bacc as bacc
    from concourse.bass_utils import run_bass_kernel_spmd

    n = {k: np.asarray(v) for k, v in inputs.items()}
    par = np.concatenate(
        [_chan(n["g_mix"][0]), _chan(n["lru_lambda"][0])] + [_chan(n["conv4_w"][0, k]) for k in range(4)]
        + [_chan(n["conv4_b"][0]), _chan(n["b_rg_r"][0].reshape(-1)), _chan(n["b_rg_i"][0].reshape(-1))]
        + [_chan(n["conv3_w"][0, k]) for k in range(3)]
        + [_chan(n["g_ffn"][0]), _chan(n["g_ple"][0]), _chan(n["g_final"]), np.full((P, 1), EPS, np.float32)]
        + [_chan(n["norm1_gain_2"][0])] + [_twice(n["nsa_q_gain_2"][0])] * A_R + [_twice(n["nsa_ks_gain_2"][0])]
        + [_twice(n["nsa_kw_gain_2"][0]), _twice(n["nsa_kc_gain_2"][0]), _chan(n["cmp_pos_2"][0].reshape(-1))]
        + [_chan(n["mla_q_lora_gain_2"][0]), _chan(n["mla_kv_lora_gain_2"][0])]
        + [_rows(n["mla_q_gain_2"][0])] * B_H + [_rows(n["mla_k_gain_2"][0])] * B_H
        + [_chan(_by_r(n["out_gain_a_2"][0][:, None])[:, 0]), _chan(n["out_gain_b_2"][0]), _chan(n["norm2_gain_2"][0])],
        axis=1)
    arrays = {
        "x_in": _feature_major(n["x"][0]), "par_in": np.ascontiguousarray(par),
        "p_in": _feature_major(n["p"][0, 0]), "cst_in": _constants(), "stream_in": _stream(n),
        "pos_in": np.ascontiguousarray(np.broadcast_to(n["positions_2"].astype(np.int32), (P, T))),
        "u_in": np.ascontiguousarray(n["peer_u_2"][0].reshape(N_KEYS, N_KEYS, DC, P).transpose(1, 3, 2, 0)
                                     .reshape(N_KEYS, P, D)),
        "v_in": np.ascontiguousarray(n["peer_v_2"][0].reshape(N_KEYS, NQ, E_Y, 2, 2, HB * P).transpose(1, 4, 2, 0, 3, 5)
                                     .reshape(NQ * 2 * E_Y, P, D)),
    }
    nc = bacc.Bacc("TRN2", target_bir_lowering=False, num_devices=1)
    aps = [nc.dram_tensor(k, a.shape, mybir.dt.from_np(a.dtype), kind="ExternalInput").ap() for k, a in arrays.items()]
    out = nc.dram_tensor("out", (P, DC, T), F32, kind="ExternalOutput").ap()
    dense = nc.dram_tensor("dense", (P, QN, T), F32, kind="Internal").ap()
    build(nc, *aps, out, dense)
    r = run_bass_kernel_spmd(nc, [arrays], core_ids=[0])
    return np.ascontiguousarray(r.results[0]["out"].transpose(1, 0, 2).reshape(D, T).T)[None]
```
